# Optimizing a Trainium2 kernel written in Bass

```python
import jax, jax.numpy as jnp
from jax import lax
import numpy as np

D_MODEL = 1024
BATCH = 1
SEQ = 1024
DEPTH = 1
DEC_BATCH = 1
DEC_SEQ = 32
PAST_LEN = 256

CHUNK = 64
EPS = 1e-6
NEG_INF = -1e30
MLA_HEADS = 8
QK_NOPE = 64
QK_ROPE = 32
V_DIM = 64
Q_RANK = 384
KV_RANK = 256
MLA_WIDTH = MLA_HEADS * V_DIM
ROPE_THETA = 10000.0
Q_BLOCK = 128
CONV_WIDTH = 512
CONV_K = 3
D_MIX = MLA_WIDTH + CONV_WIDTH
SPLITS = (Q_RANK, Q_RANK + KV_RANK, Q_RANK + KV_RANK + QK_ROPE,
          Q_RANK + KV_RANK + QK_ROPE + CONV_WIDTH,
          Q_RANK + KV_RANK + QK_ROPE + 2 * CONV_WIDTH)
D_IN = Q_RANK + KV_RANK + QK_ROPE + 3 * CONV_WIDTH
PEER_HEADS = 8
N_KEYS = 128
N_EXPERTS = N_KEYS * N_KEYS
PEER_TOPK = 16
PEER_DQ = 256
PEER_BLOCK = 128

kernel_name = "hymba_mla_shortconv_peer_stream_step"

def rmsnorm(x, g):
    xf = x.astype(jnp.float32)
    y = xf * lax.rsqrt(jnp.mean(xf * xf, axis=-1, keepdims=True) + EPS)
    return (y * g.astype(jnp.float32)).astype(x.dtype)

def rope_tables(pos):
    half = QK_ROPE // 2
    freqs = ROPE_THETA ** (-jnp.arange(half, dtype=jnp.float32) / half)
    ang = pos.astype(jnp.float32)[:, None] * freqs[None, :]
    return jnp.cos(ang), jnp.sin(ang)

def apply_rope(x, cos, sin):
    x1, x2 = jnp.split(x, 2, axis=-1)
    c = cos.astype(x.dtype)
    s = sin.astype(x.dtype)
    return jnp.concatenate([x1 * c - x2 * s, x1 * s + x2 * c], axis=-1)

def chunk_causal_attention(q, k, v, q_pos, k_pos):
    B, Sq, H, Dqk = q.shape
    qb = Q_BLOCK if Sq % Q_BLOCK == 0 else Sq
    nb = Sq // qb
    scale = Dqk ** -0.5
    k_chunk = k_pos // CHUNK
    q_blocks = q.reshape(B, nb, qb, H, Dqk).transpose(1, 0, 2, 3, 4)
    p_blocks = q_pos.reshape(nb, qb)

    def block(args):
        qblk, pblk = args
        s = jnp.einsum('bqhd,bkhd->bhqk', qblk, k,
                       preferred_element_type=jnp.float32) * scale
        mask = k_chunk[None, :] <= (pblk // CHUNK)[:, None]
        s = jnp.where(mask[None, None], s, NEG_INF)
        p = jax.nn.softmax(s, axis=-1)
        return jnp.einsum('bhqk,bkhd->bqhd', p.astype(v.dtype), v)

    out = lax.map(block, (q_blocks, p_blocks))
    return out.transpose(1, 0, 2, 3, 4).reshape(B, Sq, H, v.shape[-1])

def peer_ffn(h, w_peer_q, peer_keys, peer_u, peer_v):
    B, S, D = h.shape
    T = B * S
    n_blk = -(-T // PEER_BLOCK)
    flat = jnp.pad(h.reshape(T, D), ((0, n_blk * PEER_BLOCK - T), (0, 0)))

    def block(xb):
        q = (xb @ w_peer_q).reshape(PEER_BLOCK, PEER_HEADS, 2, PEER_DQ // 2)
        s = jnp.einsum('thcd,hcnd->thcn', q, peer_keys,
                       preferred_element_type=jnp.float32)
        s_top, i_top = lax.top_k(s, PEER_TOPK)
        cand = (s_top[:, :, 0, :, None] + s_top[:, :, 1, None, :]).reshape(
            PEER_BLOCK, PEER_HEADS, PEER_TOPK * PEER_TOPK)
        cand_idx = (i_top[:, :, 0, :, None] * N_KEYS + i_top[:, :, 1, None, :]).reshape(
            PEER_BLOCK, PEER_HEADS, PEER_TOPK * PEER_TOPK)
        best, sel = lax.top_k(cand, PEER_TOPK)
        experts = jnp.take_along_axis(cand_idx, sel, axis=-1)
        g = jax.nn.softmax(best, axis=-1)
        u = peer_u[experts]
        a = jax.nn.gelu(jnp.einsum('thkd,td->thk', u, xb), approximate=False)
        v = peer_v[experts]
        return jnp.einsum('thk,thkd->td', (g * a).astype(v.dtype), v)

    out = lax.map(block, flat.reshape(n_blk, PEER_BLOCK, D))
    return out.reshape(n_blk * PEER_BLOCK, D)[:T].reshape(B, S, D)

def layer(x, pos, past_kv, past_kpe, past_conv,
          g_attn_norm, w_in, g_q, w_uq, g_kv, w_ukv, w_conv,
          g_mla_out, g_conv_out, w_out, g_ffn_norm,
          w_peer_q, peer_keys, peer_u, peer_v):
    B, S, _ = x.shape
    h = rmsnorm(x, g_attn_norm)
    z = h @ w_in
    c_q, c_kv, k_pe, u_conv, b_gate, c_gate = jnp.split(z, SPLITS, axis=-1)
    cos, sin = rope_tables(pos)

    q = (rmsnorm(c_q, g_q) @ w_uq).reshape(B, S, MLA_HEADS, QK_NOPE + QK_ROPE)
    q_nope, q_pe = jnp.split(q, [QK_NOPE], axis=-1)
    q_pe = apply_rope(q_pe, cos[:, None, :], sin[:, None, :])
    c_kv = rmsnorm(c_kv, g_kv)
    k_pe = apply_rope(k_pe, cos, sin)
    if past_kv is None:
        kv_all, kpe_all, k_pos = c_kv, k_pe, pos
    else:
        kv_all = jnp.concatenate([past_kv, c_kv], axis=1)
        kpe_all = jnp.concatenate([past_kpe, k_pe], axis=1)
        k_pos = jnp.concatenate([jnp.arange(past_kv.shape[1], dtype=pos.dtype), pos])
    Sk = kv_all.shape[1]
    kv = (kv_all @ w_ukv).reshape(B, Sk, MLA_HEADS, QK_NOPE + V_DIM)
    k_nope, v = jnp.split(kv, [QK_NOPE], axis=-1)
    k = jnp.concatenate(
        [k_nope, jnp.broadcast_to(kpe_all[:, :, None, :], (B, Sk, MLA_HEADS, QK_ROPE))], axis=-1)
    attn = chunk_causal_attention(jnp.concatenate([q_nope, q_pe], axis=-1), k, v, pos, k_pos)
    attn = attn.reshape(B, S, MLA_WIDTH)

    u = c_gate * u_conv
    if past_conv is None:
        past_conv = jnp.zeros((B, CONV_K - 1, CONV_WIDTH), u.dtype)
    up = jnp.concatenate([past_conv, u], axis=1)
    conv = up[:, 0:S] * w_conv[0]
    for j in range(1, CONV_K):
        conv = conv + up[:, j:j + S] * w_conv[j]
    conv_out = b_gate * conv
    new_conv = up[:, -(CONV_K - 1):]

    mix = jnp.concatenate([rmsnorm(attn, g_mla_out), rmsnorm(conv_out, g_conv_out)], axis=-1)
    x = x + mix @ w_out
    x = x + peer_ffn(rmsnorm(x, g_ffn_norm), w_peer_q, peer_keys, peer_u, peer_v)
    return x, c_kv, k_pe, new_conv

def setup_inputs(seed: int = 0) -> dict:
    key = jax.random.key(seed)
    ks = jax.random.split(key, 24)
    nrm = lambda k, shape, s: jax.random.normal(k, shape, jnp.float32) * s
    gain = lambda k, shape: 1.0 + 0.02 * jax.random.normal(k, shape, jnp.float32)
    return {
        "x_prompt": nrm(ks[0], (BATCH, SEQ, D_MODEL), 1.0),
        "x_sample": nrm(ks[1], (DEC_BATCH, DEC_SEQ, D_MODEL), 1.0),
        "cache_kv_latent": nrm(ks[2], (DEPTH, DEC_BATCH, PAST_LEN, KV_RANK), 1.0),
        "cache_k_rope": nrm(ks[3], (DEPTH, DEC_BATCH, PAST_LEN, QK_ROPE), 1.0),
        "state_conv": nrm(ks[4], (DEPTH, DEC_BATCH, CONV_K - 1, CONV_WIDTH), 1.0),
        "g_attn_norm": gain(ks[5], (DEPTH, D_MODEL)),
        "w_in": nrm(ks[6], (DEPTH, D_MODEL, D_IN), D_MODEL ** -0.5),
        "g_q": gain(ks[7], (DEPTH, Q_RANK)),
        "w_uq": nrm(ks[8], (DEPTH, Q_RANK, MLA_HEADS * (QK_NOPE + QK_ROPE)), Q_RANK ** -0.5),
        "g_kv": gain(ks[9], (DEPTH, KV_RANK)),
        "w_ukv": nrm(ks[10], (DEPTH, KV_RANK, MLA_HEADS * (QK_NOPE + V_DIM)), KV_RANK ** -0.5),
        "w_conv": nrm(ks[11], (DEPTH, CONV_K, CONV_WIDTH), CONV_K ** -0.5),
        "g_mla_out": gain(ks[12], (DEPTH, MLA_WIDTH)),
        "g_conv_out": gain(ks[13], (DEPTH, CONV_WIDTH)),
        "w_out": nrm(ks[14], (DEPTH, D_MIX, D_MODEL), D_MIX ** -0.5),
        "g_ffn_norm": gain(ks[15], (DEPTH, D_MODEL)),
        "w_peer_q": nrm(ks[16], (DEPTH, D_MODEL, PEER_HEADS * PEER_DQ), D_MODEL ** -0.5),
        "peer_keys": nrm(ks[17], (DEPTH, PEER_HEADS, 2, N_KEYS, PEER_DQ // 2), (PEER_DQ // 2) ** -0.5),
        "peer_u": nrm(ks[18], (DEPTH, N_EXPERTS, D_MODEL), D_MODEL ** -0.5),
        "peer_v": nrm(ks[19], (DEPTH, N_EXPERTS, D_MODEL), PEER_HEADS ** -0.5),
        "g_final": gain(ks[20], (D_MODEL,)),
    }

def reference(x_prompt, x_sample, cache_kv_latent, cache_k_rope, state_conv,
              g_attn_norm, w_in, g_q, w_uq, g_kv, w_ukv, w_conv,
              g_mla_out, g_conv_out, w_out, g_ffn_norm,
              w_peer_q, peer_keys, peer_u, peer_v, g_final):
    pos_p = jnp.arange(x_prompt.shape[1], dtype=jnp.int32)
    pos_s = cache_kv_latent.shape[2] + jnp.arange(x_sample.shape[1], dtype=jnp.int32)
    hp, hs = x_prompt, x_sample
    kv_p, kpe_p, conv_p, kv_s, kpe_s, conv_s = [], [], [], [], [], []
    for l in range(DEPTH):
        params = (g_attn_norm[l], w_in[l], g_q[l], w_uq[l], g_kv[l], w_ukv[l], w_conv[l],
                  g_mla_out[l], g_conv_out[l], w_out[l], g_ffn_norm[l],
                  w_peer_q[l], peer_keys[l], peer_u[l], peer_v[l])
        hp, a, b, c = layer(hp, pos_p, None, None, None, *params)
        kv_p.append(a); kpe_p.append(b); conv_p.append(c)
        hs, a, b, c = layer(hs, pos_s, cache_kv_latent[l], cache_k_rope[l], state_conv[l], *params)
        kv_s.append(a); kpe_s.append(b); conv_s.append(c)
    y_prompt = rmsnorm(hp, g_final)
    y_sample = rmsnorm(hs, g_final)
    return (y_prompt, y_sample,
            jnp.stack(kv_p), jnp.stack(kpe_p), jnp.stack(conv_p),
            jnp.stack(kv_s), jnp.stack(kpe_s), jnp.stack(conv_s))


_drawn_inputs = setup_inputs


def setup_inputs(seed=0):
    import zlib

    import numpy as np

    out = dict(_drawn_inputs(seed))
    spreads = {}
    factors = {'g_q': 3.389,
     'g_mla_out': 10.538,
     'g_conv_out': 9.952,
     'g_ffn_norm': 10.153,
     'g_final': 8.727}
    for name, (base, spread) in spreads.items():
        noise = np.random.default_rng([zlib.crc32(name.encode()), seed]).standard_normal(out[name].shape)
        drawn = base * np.exp(spread * noise) if base else spread * noise
        out[name] = __import__('jax').numpy.asarray(drawn.astype(out[name].dtype))
    for name, factor in factors.items():
        out[name] = (out[name] * factor).astype(out[name].dtype)
    return out
```

```python
from contextlib import ExitStack

import numpy as np
import concourse.bass as bass
from concourse import mybir

F32 = mybir.dt.float32
U32 = mybir.dt.uint32
ALU = mybir.AluOpType
ACT = mybir.ActivationFunctionType
AX = mybir.AxisListType

P = 128
D = 1024
KC = D // P
SEQ, DEC, PAST = 1024, 32, 256
TILES = SEQ // P
S_TILE = TILES
CHUNK = 64
EPS = 1e-6
NEG = -1e30
LOWEST = -3.0e38
H, NOPE, ROPE, VD = 8, 64, 32, 64
QK = NOPE + ROPE
HALF = ROPE // 2
SCALE = float(QK) ** -0.5
QR, KVR, CW, CK = 384, 256, 512, 3
QC, CC = QR // P, CW // P
NATW = QR + KVR + ROPE
NKEYS, TOPK, PH = 128, 16, 8
NEXP = NKEYS * NKEYS
SLOTS = PH * TOPK
KEYS = SEQ
KB = KEYS // P

NAT_BLOCKS = 6
IN_BLOCKS = NAT_BLOCKS + 3 * CC
PQ_BLOCKS = 2 * PH
BLOCKS = IN_BLOCKS + PQ_BLOCKS
WBUF = 2
RING = 4
LEAD = 2 * RING
PACK = P // DEC
PSLOTS = SLOTS // PACK

BLOCK_STEP = [4 + 2 * b for b in range(IN_BLOCKS)] + [86 + 2 * b for b in range(PQ_BLOCKS)]
ATT_STEP = 42
ACT_FRONT = 5
DVE_FRONT = 186

C_GATTN, C_GQ, C_GMLA, C_GCONV, C_WCONV, C_STATE = 0, 8, 11, 15, 19, 31
NCOLS = 39


def first(t):
    return isinstance(t, int) and t == 0


def sample(t):
    return isinstance(t, int) and t == S_TILE


class Count:

    def __init__(self, sem, per):
        self.sem, self.per = sem, per

    def start(self, t):
        self.t, self.n = t, 0

    def link(self, eng, ins, wait=None):
        self.n += 1
        ins.then_inc(self.sem, 1)
        (wait or type(eng).wait_ge)(eng, self.sem, self.per * self.t + self.n)

    def end(self):
        assert self.n == self.per, (self.n, self.per)


def build(nc, a):
    with ExitStack() as ctx:
        def sb(name, cols, dt=F32):
            return ctx.enter_context(nc.sbuf_tensor(name, [P, cols], dt))

        def psum(name):
            return ctx.enter_context(nc.psum_tensor(name, [P, 512], F32))

        def sem(name):
            return ctx.enter_context(nc.semaphore(name))

        w_out = sb("w_out_sb", KC * D)
        w_uq = sb("w_uq_sb", QC * H * QK)
        w_ukv = sb("w_ukv_sb", 2 * H * (NOPE + VD))
        keysT = sb("keysT_sb", PQ_BLOCKS * NKEYS)
        g_ffn = sb("g_ffn_sb", D)
        g_fin = sb("g_fin_sb", D)
        g_kv = sb("g_kv_sb", KVR)
        cols = sb("cols_sb", NCOLS)
        kT = sb("kT", H * KEYS)
        vv = sb("vv", KB * H * VD)
        wst = [sb(f"wst{i}", KC * P) for i in range(WBUF)]
        ring = [sb(f"ring{i}", 2 * D) for i in range(RING)]
        x_front = sb("x_front", D)
        x_peer = sb("x_peer", D)
        hf_front = sb("hf_front", D)
        hf_peer = sb("hf_peer", D)
        idx_front = sb("idx_front", SLOTS, U32)
        idx_peer = sb("idx_peer", SLOTS, U32)
        idx_lead = sb("idx_lead", LEAD, U32)
        gate_front = sb("gate_front", SLOTS)
        gate_peer = sb("gate_peer", SLOTS)
        rope = sb("rope", ROPE)
        actT = sb("actT", KC * P)
        ckn = sb("ckn", KVR + ROPE)
        qT = sb("qT", H * P)
        cqT = qT[:, 0:QR]
        ckT = qT[:, QR:QR + KVR]
        uT = sb("uT", CC * (P + CK - 1))
        convT = sb("convT", CW)
        attn = convT
        convp = sb("convp", CC * (CK - 1))
        csb = sb("csb", 2 * P)
        mask = sb("mask", KEYS)
        mask_tile = sb("mask_tile", P)
        zeros = sb("zeros", P)
        ident = sb("ident", P)
        fold = sb("fold", DEC)
        ones = sb("ones", 1)
        bufA = sb("bufA", D)
        bufB = sb("bufB", D)
        diag = sb("diag", 2 * P)
        rtmp = bufA[:, D - 4 * H * HALF:D]
        tv = sb("tv", PQ_BLOCKS * TOPK)
        ti = sb("ti", PQ_BLOCKS * TOPK, U32)
        tif = sb("tif", 2 * TOPK)
        best = sb("best", SLOTS)
        pos = sb("pos", TOPK, U32)
        pab = sb("pab", 2 * TOPK, U32)
        pabf = sb("pabf", 2 * TOPK)
        eab = sb("eab", 2 * TOPK)
        iota16 = sb("iota16", TOPK)
        gsum = sb("gsum", 2 * PH)
        dots = sb("dots", SLOTS)
        gl = sb("gl", SLOTS)
        wk = sb("wk", SLOTS)
        st = sb("st", 24)
        mx = sb("mx", H)
        nm = sb("nm", H)
        rs = sb("rs", H)
        ri = sb("ri", H)

        acc = ctx.enter_context(nc.psum_tensor("acc", [P, 2 * 512], F32))
        Sps = ctx.enter_context(nc.psum_tensor("Sps", [P, 2 * 512], F32))
        S0, S1 = Sps[:, 0:512], Sps[:, 512:1024]
        T0, T1, M0, M1 = [psum(n) for n in ("T0", "T1", "M0", "M1")]

        s_passed = {e: sem(f"s_passed_{e}") for e in ("pool", "dve")}

        def wait_apart(eng, s, value):
            eng.wait_ge(s, value)
            eng.sem_inc(s_passed["pool" if eng is nc.gpsimd else "dve"], 1)

        s_const = sem("s_const")
        s_const2 = sem("s_const2")
        s_x = sem("s_x_loaded")
        s_rope = sem("s_rope_loaded")
        s_w = [sem(f"s_w_loaded{i}") for i in range(WBUF)]
        s_wused = sem("s_w_used")
        s_past = sem("s_past_loaded")
        s_kvst = sem("s_kv_stored")
        s_cpst = sem("s_conv_stored")
        s_yst = sem("s_y_stored")
        s_g = [sem(f"s_gathered{i}") for i in range(RING)]
        s_init = sem("s_init")
        s_fold = sem("s_fold")
        s_ropeb = sem("s_rope_used")
        s_ssx = sem("s_ssx")
        s_rx = sem("s_rx")
        s_h = sem("s_h")
        s_hps = sem("s_h_turned")
        s_hT = sem("s_hT")
        s_ssz = sem("s_ssz")
        s_rz = sem("s_rz")
        s_cqn = sem("s_cqn")
        s_ckn = sem("s_ckn")
        s_cqps = sem("s_cq_turned")
        s_cqT = sem("s_cqT")
        s_ckps = sem("s_ck_turned")
        s_ckT = sem("s_ckT")
        s_kpe = sem("s_kpe")
        s_kvps = sem("s_kv_ps")
        s_kv = sem("s_kv_kept")
        s_qps = sem("s_q_ps")
        s_qn = sem("s_qn")
        s_qr = sem("s_q_rotated")
        s_qTps = sem("s_q_turned")
        s_qT = sem("s_qT")
        s_ucb = sem("s_ucb")
        s_c = sem("s_c")
        s_conv = sem("s_conv")
        s_carry = sem("s_carry")
        s_csq = sem("s_csq")
        s_mixc = sem("s_mixc")
        s_css = sem("s_css")
        s_ssc = sem("s_ssc")
        s_rc = sem("s_rc")
        s_mask = sem("s_mask")
        s_sc = sem("s_scores")
        s_sm = sem("s_masked")
        s_nm = sem("s_negmax")
        s_p = sem("s_probs")
        s_pTps = sem("s_p_turned")
        s_pTa = sem("s_pT_low")
        s_pTb = sem("s_pT_high")
        s_pv = sem("s_pv")
        s_at = sem("s_attn")
        s_ssa = sem("s_ssa")
        s_aps = sem("s_attn_turned")
        s_mixa = sem("s_mixa")
        s_wo = sem("s_wo")
        s_xm = sem("s_xmid")
        s_ssm = sem("s_ssm")
        s_hf = sem("s_hf")
        s_hfps = sem("s_hf_turned")
        s_hfT = sem("s_hfT")
        s_pq = sem("s_pq")
        s_pqT = sem("s_pqT")
        s_s = sem("s_keyscores")
        s_l1 = sem("s_level1")
        s_idx = sem("s_idx")
        s_best = sem("s_best")
        s_ge = sem("s_gate_exp")
        s_gate = sem("s_gate")
        s_handx = sem("s_hand_x")
        s_handh = sem("s_hand_hf")
        s_handg = sem("s_hand_gate")
        s_handi = sem("s_hand_idx")
        s_pack = sem("s_packed")
        s_dot = sem("s_dot")
        s_diag = sem("s_diag")
        s_slot = sem("s_slot_done")
        s_x2 = sem("s_x2")
        s_ss2 = sem("s_ss2")
        s_y = sem("s_y")
        dve_f = Count(sem("s_dve_front"), DVE_FRONT)
        act_f = Count(sem("s_act_front"), ACT_FRONT)
        act_y = Count(sem("s_act_final"), 1)
        act_p = Count(sem("s_act_peer"), 2 * SLOTS)
        dve_y = Count(sem("s_dve_final"), 2)

        w_out_v = w_out[:, :].rearrange("p (k n) -> p k n", k=KC)
        w_uq_v = w_uq[:, :].rearrange("p (k n) -> p k n", k=QC)
        w_ukv_v = w_ukv[:, :].rearrange("p (k h c) -> p k h c", k=2, h=H)
        keysT_v = keysT[:, :].rearrange("p (b n) -> p b n", b=PQ_BLOCKS)
        wst_v = [w[:, :].rearrange("p (k n) -> p k n", k=KC) for w in wst]
        kT_v = kT[:, :].rearrange("p (h k) -> p h k", h=H)
        actT_v = actT[:, :].rearrange("p (k n) -> p k n", k=KC)
        uT_v = uT[:, :].rearrange("p (j n) -> p j n", j=CC)
        conv_v = convT[:, :].rearrange("p (j n) -> p j n", j=CC)
        state_v = cols[:, C_STATE:C_STATE + 8].rearrange("p (j n) -> p j n", j=CC)
        past = bufA[:, 448:1024].rearrange("p (b n) -> p b n", b=2)
        csq = bufA[:, 384:896].rearrange("p (j n) -> p j n", j=CC)
        hnat = bufA
        cqn = bufA[:, 0:QR]
        qn = bufB[:, 0:H * QK]
        pqT = bufB[:, 0:2 * P]
        s2 = bufA[:, 0:128]
        cand = bufA[:, 128:384]
        cand2 = bufA[:, 384:640]
        hot = bufA[:, 640:896].rearrange("p (k c) -> p k c", c=TOPK)
        Sb = [S0, S1]
        Tb = [T0, T1]
        Mb = [M0, M1]
        SSX, RX, SSQ, RQ, SSK, RK, RC, SSA, RA, SSM, RM, SS2, R2, SSC, EPSC = range(15)

        def col(c):
            return st[:, c:c + 1]

        def gain(c, n):
            return cols[:, c:c + n].unsqueeze(2).to_broadcast([P, n, P])

        def v3(ap, n):
            return ap.rearrange("p (k n) -> p k n", k=n)

        block = ctx.enter_context(nc.Block())

        @block.sync
        def _(sp):
            def load_block(t, b):
                if b >= WBUF or not isinstance(t, int) or t > 0:
                    sp.wait_ge(s_wused, BLOCKS * t + b - WBUF + 1)
                if b == NAT_BLOCKS - 1:
                    sp.dma_start(wst_v[b % WBUF][:, :, 0:ROPE],
                                 a["w_nar"].rearrange("p (k n) -> p k n", k=KC)).then_inc(s_w[b % WBUF], 16)
                else:
                    sp.dma_start(wst[b % WBUF][:, :], a["w_str"][b - (b >= NAT_BLOCKS)]).then_inc(s_w[b % WBUF], 16)

            def front(t, k):
                if k == 0:
                    if not first(t):
                        sp.wait_ge(s_handx, t)
                    if sample(t):
                        sp.dma_start(x_front[0:DEC, :], a["x_s"]).then_inc(s_x, 16)
                    else:
                        sp.dma_start(x_front[:, :], a["x_p"][bass.ds(t * P, P), :]).then_inc(s_x, 16)
                    if not first(t):
                        sp.wait_ge(s_ropeb, 1 * t)
                    sp.dma_start(rope[:, :], a["rope"][bass.ds(t * P, P), :]).then_inc(s_rope, 16)
                for b in range(BLOCKS):
                    if max(0, BLOCK_STEP[b] - 4) == k:
                        load_block(t, b)
                if sample(t) and k == 4:
                    sp.wait_ge(s_hps, 2 * t + 2)
                    sp.dma_start(past[:, :, 0:KVR], a["c_kv"].rearrange("(b p) n -> p b n", p=P)).then_inc(s_past, 16)
                    sp.dma_start(past[:, :, KVR:KVR + ROPE],
                                 a["c_pe"].rearrange("(b p) n -> p b n", p=P)).then_inc(s_past, 16)
                if k == 17:
                    sp.wait_ge(s_ckn, t + 1)
                    if sample(t):
                        sp.dma_start(a["o_kv_s"], ckn[0:DEC, 0:KVR]).then_inc(s_kvst, 16)
                        sp.dma_start(a["o_pe_s"], ckn[0:DEC, KVR:KVR + ROPE]).then_inc(s_kvst, 16)
                    else:
                        sp.dma_start(a["o_kv_p"][bass.ds(t * P, P), :], ckn[:, 0:KVR]).then_inc(s_kvst, 16)
                        sp.dma_start(a["o_pe_p"][bass.ds(t * P, P), :], ckn[:, KVR:KVR + ROPE]).then_inc(s_kvst, 16)
                if k == 40 and sample(t):
                    sp.wait_ge(s_carry, S_TILE + 1)
                    sp.dma_start(a["o_cv_p"], convp[:, :]).then_inc(s_cpst, 16)
                    sp.wait_ge(s_conv, CC * (t + 1))
                    sp.dma_start(a["o_cv_s"].rearrange("p (j n) -> p j n", j=CC),
                                 uT_v[:, :, DEC:DEC + CK - 1]).then_inc(s_cpst, 16)

            def store_y(t):
                sp.wait_ge(s_y, t + 1)
                if sample(t):
                    sp.dma_start(a["o_y_s"], x_peer[0:DEC, :]).then_inc(s_yst, 16)
                else:
                    sp.dma_start(a["o_y_p"][bass.ds(t * P, P), :], x_peer[:, :]).then_inc(s_yst, 16)

            sp.dma_start(cols[:, :], a["cols"]).then_inc(s_const, 16)
            front(0, 0)
            for dst, src in ((g_kv, a["g_kv"].partition_broadcast(P)), (w_uq, a["w_uq"]), (w_ukv, a["w_ukv"])):
                sp.dma_start(dst[:, :], src).then_inc(s_const, 16)
            for k in range(1, SLOTS):
                front(0, k)
                if k == 14:
                    for dst, src in ((w_out, a["w_out"]), (g_ffn, a["g_ffn"].partition_broadcast(P)),
                                     (keysT, a["keysT"]), (g_fin, a["g_fin"].partition_broadcast(P))):
                        sp.dma_start(dst[:, :], src).then_inc(s_const2, 16)
            with sp.Fori(0, TILES - 1) as t:
                for k in range(SLOTS):
                    front(t + 1, k)
                store_y(t)
            for k in range(SLOTS):
                front(S_TILE, k)
            store_y(TILES - 1)
            sp.wait_ge(s_slot, SLOTS * TILES + RING)
            sp.wait_ge(s_idx, PH * (S_TILE + 1))
            sp.wait_ge(s_gate, S_TILE + 1)
            for q in range(PACK):
                rows = slice(q * DEC, (q + 1) * DEC)
                part = slice(q * PSLOTS, (q + 1) * PSLOTS)
                sp.dma_start(idx_peer[rows, 0:PSLOTS], idx_front[0:DEC, part]).then_inc(s_pack, 16)
                sp.dma_start(gate_peer[rows, 0:PSLOTS], gate_front[0:DEC, part]).then_inc(s_pack, 16)
                sp.dma_start(hf_peer[rows, :], hf_front[0:DEC, :]).then_inc(s_pack, 16)
            store_y(S_TILE)
            sp.wait_ge(s_yst, 16 * (S_TILE + 1))
            sp.wait_ge(s_kvst, 32 * (S_TILE + 1))
            sp.wait_ge(s_cpst, 32)

        @block.gpsimd
        def _(pool):
            pool.memset(ident[:, :], 0.0).then_inc(s_init, 1)
            pool.memset(mask_tile[:, :], 0.0).then_inc(s_init, 1)
            pool.memset(ones[:, :], 1.0).then_inc(s_init, 1)
            pool.memset(zeros[:, :], 0.0).then_inc(s_init, 1)
            pool.iota(iota16[:, :], pattern=[[1, TOPK]], base=0, channel_multiplier=0,
                      allow_small_or_imprecise_dtypes=True).then_inc(s_init, 1)
            pool.wait_ge(s_init, 5)
            pool.affine_select(out=ident[:, :], in_=ident[:, :], compare_op=ALU.not_equal, fill=1.0, base=0,
                               pattern=[[-1, P]], channel_multiplier=1).then_inc(s_init, 1)
            pool.memset(mask_tile[0:CHUNK, CHUNK:P], NEG).then_inc(s_init, 1)
            pool.sem_inc(s_slot, RING)
            pool.memset(col(EPSC), EPS).then_inc(s_init, 1)
            pool.memset(kT[:, :], 0.0).then_inc(s_init, 1)
            pool.memset(vv[:, :], 0.0).then_inc(s_init, 1)
            pool.memset(mask[:, :], NEG).then_inc(s_init, 1)

            def gather(tile, k, before, lead=LEAD):
                wait_apart(pool, s_slot, before + k + 1)
                pool.indirect_dma_start(ring[k % RING][:, :], None, a["uv"],
                                        bass.IndirectOffsetOnAxis(ap=(idx_lead if k < lead else idx_peer)[:, k:k + 1], axis=0)
                                        ).then_inc(s_g[k % RING], 16)
                if k < lead and k == RING - 1:
                    pool.tensor_copy(idx_peer[:, LEAD:SLOTS], idx_front[:, LEAD:SLOTS]).then_inc(s_handi, 1)
                if k == lead - 1:
                    wait_apart(pool, s_handi, 2 * tile + 2)

            def hand(t):
                wait_apart(pool, s_idx, PH * (t + 1))
                pool.tensor_copy(idx_lead[:, :], idx_front[:, 0:LEAD]).then_inc(s_handi, 1)
                wait_apart(pool, s_handi, 2 * t + 1)

            hand(0)
            with pool.Fori(0, TILES - 1) as t:
                for k in range(SLOTS):
                    gather(t, k, SLOTS * t)
                hand(t + 1)
            for k in range(SLOTS):
                gather(TILES - 1, k, SLOTS * (TILES - 1))
            pool.wait_ge(s_pack, 16 * 3 * PACK)
            for k in range(PSLOTS):
                gather(S_TILE, k, SLOTS * TILES, lead=0)

        @block.tensor
        def _(pe):
            def turn(dst, src, rows=P):
                return pe.transpose(dst, src, ident[:, :])

            def w_ready(t, b):
                pe.wait_ge(s_w[b % WBUF], 16 * ((BLOCKS // WBUF) * t + b // WBUF + 1))

            def in_block(t, b):
                w_ready(t, b)
                w = wst_v[b % WBUF]
                if b < NAT_BLOCKS:
                    n = ROPE if b == NAT_BLOCKS - 1 else P
                    bank = Mb[b // QC]
                    at = (b % QC) * P
                    if b % QC == 0 and not first(t):
                        pe.wait_ge(s_pqT, PQ_BLOCKS * t)
                    for c in range(KC):
                        mm = pe.matmul(bank[:, at:at + n], actT_v[:, c, :], w[:, c, 0:n],
                                       start=(c == 0), stop=(c == KC - 1))
                    mm.then_inc(s_wused, 1)
                else:
                    j, part = divmod(b - NAT_BLOCKS, 3)
                    bank = Sb[j % 2]
                    if part == 0:
                        if j >= 2:
                            pe.wait_ge(s_conv, CC * t + j - 1)
                        elif not first(t):
                            pe.wait_ge(s_l1, PQ_BLOCKS * t)
                    for c in range(KC):
                        mm = pe.matmul(bank[:, part * P:(part + 1) * P], w[:, c, :], actT_v[:, c, :],
                                       start=(c == 0), stop=(c == KC - 1))
                    mm.then_inc(s_wused, 1)

            def kv_stage(n, src, k):
                if k == 0:
                    if not first(n):
                        pe.wait_ge(s_kv, 3 * n)
                    for i, (lo, hi) in enumerate(((0, P), (P, 2 * P), (KVR + ROPE - QK, KVR + ROPE))):
                        mm = turn(T1[0:hi - lo, i * P:(i + 1) * P], src[:, lo:hi])
                    mm.then_inc(s_ckps, 1)
                if k == 1:
                    pe.wait_ge(s_ckT, n + 1)
                    pe.wait_ge(s_kpe, n + 1)
                    for half in range(2):
                        for h in range(4):
                            for c in range(2):
                                mm = pe.matmul(Tb[half][0:NOPE, h * P:(h + 1) * P], w_ukv_v[:, c, 4 * half + h, 0:NOPE],
                                               ckT[:, c * P:(c + 1) * P], start=(c == 0), stop=(c == 1))
                        mm.then_inc(s_kvps, 1)
                if k == 2:
                    pe.wait_ge(s_kv, 3 * n + 1)
                    for c in range(2):
                        mm = pe.matmul(T0[:, :].rearrange("p (h c) -> p h c", h=H), ckT[:, c * P:(c + 1) * P],
                                       w_ukv_v[:, c, :, NOPE:NOPE + VD], start=(c == 0), stop=(c == 1))
                    mm.then_inc(s_kvps, 1)

            def front(t, k):
                n = S_TILE + 2 if sample(t) else t
                if k == 3:
                    pe.wait_ge(s_h, t + 1)
                    if first(t):
                        pe.wait_ge(s_init, 11)
                        pe.wait_ge(s_const, 16 * 4)
                    for c in range(KC):
                        mm = turn(Tb[c // 4][:, (c % 4) * P:(c % 4 + 1) * P], hnat[:, c * P:(c + 1) * P])
                        if c % 4 == 3:
                            mm.then_inc(s_hps, 1)
                if k == BLOCK_STEP[0]:
                    pe.wait_ge(s_hT, 2 * t + 2)
                if sample(t):
                    if k == 7:
                        pe.wait_ge(s_past, 32)
                        kv_stage(TILES, past[:, 0, :], 0)
                    if k == 8:
                        kv_stage(TILES, past[:, 0, :], 1)
                        kv_stage(TILES, past[:, 0, :], 2)
                    if k == 9:
                        kv_stage(TILES + 1, past[:, 1, :], 0)
                    if k == 10:
                        kv_stage(TILES + 1, past[:, 1, :], 1)
                        kv_stage(TILES + 1, past[:, 1, :], 2)
                if k == 11:
                    pe.wait_ge(s_cqn, t + 1)
                    if sample(t):
                        pe.wait_ge(s_kv, 3 * n)
                    for c in range(QC):
                        mm = turn(T0[:, c * P:(c + 1) * P], cqn[:, c * P:(c + 1) * P])
                    mm.then_inc(s_cqps, 1)
                if k == 17:
                    pe.wait_ge(s_ckn, t + 1)
                    kv_stage(n, ckn, 0)
                if k in (19, 20):
                    if k == 19:
                        pe.wait_ge(s_cqT, t + 1)
                    half = k - 19
                    for c in range(QC):
                        mm = pe.matmul(Mb[half][:, 0:QR], cqT[:, c * P:(c + 1) * P],
                                       w_uq_v[:, c, half * QR:(half + 1) * QR], start=(c == 0), stop=(c == QC - 1))
                    mm.then_inc(s_qps, 1)
                if k == 21:
                    kv_stage(n, ckn, 1)
                if k == 23:
                    kv_stage(n, ckn, 2)
                if k == 25:
                    pe.wait_ge(s_qr, t + 1)
                    for h in range(H):
                        mm = turn(Mb[h // 4][0:QK, (h % 4) * P:(h % 4 + 1) * P], qn[:, h * QK:(h + 1) * QK])
                        if h % 4 == 3:
                            mm.then_inc(s_qTps, 1)
                for b in range(IN_BLOCKS):
                    if BLOCK_STEP[b] == k:
                        in_block(t, b)
                if k == 41:
                    pe.wait_ge(s_csq, t + 1)
                    pe.wait_ge(s_kv, 3 * n + 3)
                    for j in range(CC):
                        mm = pe.matmul(T1[:, 0:1], csq[:, j, :], ones[:, 0:1], start=(j == 0), stop=(j == CC - 1))
                    mm.then_inc(s_css, 1)
                for h in range(H):
                    k0 = ATT_STEP + 4 * h
                    if k == k0:
                        if h == 0:
                            pe.wait_ge(s_qT, 2 * t + 2)
                            pe.wait_ge(s_conv, CC * t + CC)
                        else:
                            pe.wait_ge(s_sm, H * t + h)
                        for half in range(2):
                            mm = pe.matmul(Sb[half][:, :], qT[0:QK, h * P:(h + 1) * P],
                                           kT_v[0:QK, h, half * 512:(half + 1) * 512], start=True, stop=True)
                        mm.then_inc(s_sc, 1)
                    if k == k0 + 2:
                        pe.wait_ge(s_p, H * t + h + 1)
                        if h == 0:
                            pe.wait_ge(s_rc, t + 1)
                        else:
                            pe.wait_ge(s_pTa, H * t + h)
                            pe.wait_ge(s_pTb, H * t + h)
                        for c in range(KB):
                            mm = turn(Tb[c // 4][:, (c % 4) * P:(c % 4 + 1) * P], bufA[:, c * P:(c + 1) * P])
                            if c % 4 == 3:
                                mm.then_inc(s_pTps, 1)
                    if k == k0 + 3:
                        pe.wait_ge(s_pTa, H * t + h + 1)
                        pe.wait_ge(s_pTb, H * t + h + 1)
                        for c in range(KB):
                            mm = pe.matmul(M1[:, h * VD:(h + 1) * VD], bufB[:, c * P:(c + 1) * P],
                                           vv[:, (c * H + h) * VD:(c * H + h + 1) * VD],
                                           start=(c == 0), stop=(c == KB - 1))
                        mm.then_inc(s_pv, 1)
                if k == 76:
                    pe.wait_ge(s_at, t + 1)
                    for c in range(4):
                        mm = turn(T0[:, c * P:(c + 1) * P], attn[:, c * P:(c + 1) * P])
                    mm.then_inc(s_aps, 1)
                if 78 <= k < 82:
                    i = k - 78
                    if i == 0:
                        pe.wait_ge(s_mixa, t + 1)
                        if first(t):
                            pe.wait_ge(s_const2, 16 * 4)
                        pe.wait_ge(s_mixc, t + 1)
                        pe.wait_ge(s_sm, H * t + H)
                    bank = (S0, S1, T1, M0)[i]
                    for c in range(4):
                        mm = pe.matmul(bank[:, :], actT_v[:, 4 * (i % 2) + c, :],
                                       w_out_v[:, 4 * (i % 2) + c, (i // 2) * 512:(i // 2 + 1) * 512],
                                       start=(c == 0), stop=(c == 3))
                    mm.then_inc(s_wo, 1)
                if k == 84:
                    pe.wait_ge(s_hf, t + 1)
                    for c in range(KC):
                        mm = turn(Tb[c // 4][:, (c % 4) * P:(c % 4 + 1) * P], hf_front[:, c * P:(c + 1) * P])
                        if c % 4 == 3:
                            mm.then_inc(s_hfps, 1)
                for b in range(PQ_BLOCKS):
                    if k == BLOCK_STEP[IN_BLOCKS + b]:
                        if b == 0:
                            pe.wait_ge(s_hfT, 2 * t + 2)
                        if b >= 2:
                            pe.wait_ge(s_pqT, PQ_BLOCKS * t + b - 1)
                        w_ready(t, IN_BLOCKS + b)
                        w = wst_v[(IN_BLOCKS + b) % WBUF]
                        for c in range(KC):
                            mm = pe.matmul(Mb[b % 2][:, 0:P], w[:, c, :], actT_v[:, c, :],
                                           start=(c == 0), stop=(c == KC - 1))
                        mm.then_inc(s_wused, 1)
                    if k == BLOCK_STEP[IN_BLOCKS + b] + 1:
                        pe.wait_ge(s_pqT, PQ_BLOCKS * t + b + 1)
                        if b >= 2:
                            pe.wait_ge(s_l1, PQ_BLOCKS * t + b - 1)
                        pe.matmul(Sb[b % 2][:, 0:P], pqT[:, (b % 2) * P:(b % 2 + 1) * P],
                                  keysT_v[:, b, :], start=True, stop=True).then_inc(s_s, 1)

            def slot(before, k, n, rows):
                pe.wait_ge(s_diag, before + k + 1)
                for half in range(2):
                    mm = pe.matmul(acc[0:rows, half * 512:(half + 1) * 512], diag[:, (k % 2) * P:(k % 2) * P + rows],
                                   ring[k % RING][:, D + half * 512:D + (half + 1) * 512],
                                   start=(k == 0), stop=(k == n - 1))
                mm.then_inc(s_slot, 1)

            for k in range(SLOTS):
                front(0, k)
            with pe.Fori(0, TILES - 1) as t:
                for k in range(SLOTS):
                    slot(SLOTS * t, k, SLOTS, P)
                    front(t + 1, k)
                pe.wait_ge(s_x2, t + 1)
            for k in range(SLOTS):
                slot(SLOTS * (TILES - 1), k, SLOTS, P)
                front(S_TILE, k)
            pe.wait_ge(s_x2, TILES)
            for k in range(PSLOTS):
                slot(SLOTS * TILES, k, PSLOTS, DEC)

        @block.scalar
        def _(act):
            def copy(out, in_, scale=1.0):
                return act.activation(out, in_, ACT.Copy, scale=scale)

            def root(src, n, c, count, junk):
                count.link(act, act.activation(junk, src, ACT.Square, accum_out=col(c)))
                return act.activation(col(c), col(c), ACT.Sqrt, bias=col(EPSC), scale=1.0 / n)

            def kv_stage(n, at, k):
                if k == 0:
                    act.wait_ge(s_ckT, n + 1)
                    copy(kT_v[NOPE:QK, :, bass.ds(at * P, P)],
                         T1[NOPE:QK, 2 * P:3 * P].unsqueeze(1).to_broadcast([ROPE, H, P])).then_inc(s_kpe, 1)
                if k == 1:
                    for half in range(2):
                        act.wait_ge(s_kvps, 3 * n + half + 1)
                        copy(kT_v[0:NOPE, 4 * half:4 * half + 4, bass.ds(at * P, P)],
                             v3(Tb[half][0:NOPE, :], 4)).then_inc(s_kv, 1)
                if k == 2:
                    act.wait_ge(s_kvps, 3 * n + 3)
                    copy(vv[:, bass.ds(at * 512, 512)], T0[:, :]).then_inc(s_kv, 1)

            def front(t, k):
                n = S_TILE + 2 if sample(t) else t
                at = PAST // P if sample(t) else t
                if k == 0:
                    act_f.start(t)
                    if first(t):
                        act.wait_ge(s_init, 11)
                if k == 1:
                    act.wait_ge(s_x, 16 * (t + 1))
                    root(x_front[:, :], D, SSX, act_f, bufB[:, :]).then_inc(s_ssx, 1)
                if k == 2:
                    act.wait_ge(s_rx, t + 1)
                    copy(hnat[:, :], x_front[:, :], col(RX)).then_inc(s_h, 1)
                if sample(t):
                    if k == 7:
                        kv_stage(TILES, 0, 0)
                    if k == 8:
                        kv_stage(TILES, 0, 1)
                        kv_stage(TILES, 0, 2)
                    if k == 9:
                        kv_stage(TILES + 1, 1, 0)
                    if k == 10:
                        kv_stage(TILES + 1, 1, 1)
                        kv_stage(TILES + 1, 1, 2)
                if k == BLOCK_STEP[2]:
                    act.wait_ge(s_wused, BLOCKS * t + 3)
                    root(M0[:, 0:QR], QR, SSQ, act_f, bufB[:, 0:QR]).then_inc(s_ssz, 1)
                if k == BLOCK_STEP[2] + 1:
                    act.wait_ge(s_rz, t + 1)
                    copy(cqn, M0[:, 0:QR], col(RQ)).then_inc(s_cqn, 1)
                if k == BLOCK_STEP[5]:
                    act.wait_ge(s_wused, BLOCKS * t + 6)
                    root(M1[:, 0:KVR], KVR, SSK, act_f, bufB[:, QR:QR + KVR]).then_inc(s_ssz, 1)
                if k == 17:
                    if first(t):
                        act.wait_ge(s_init, 11)
                    kv_stage(n, at, 0)
                if k in (19, 20):
                    act.wait_ge(s_qps, 2 * t + k - 18)
                    copy(qn[:, (k - 19) * QR:(k - 18) * QR], Mb[k - 19][:, 0:QR]).then_inc(s_qn, 1)
                if k == 21:
                    kv_stage(n, at, 1)
                if k == 23:
                    kv_stage(n, at, 2)
                for j in range(CC):
                    if k == BLOCK_STEP[NAT_BLOCKS + 3 * j + 2]:
                        act.wait_ge(s_wused, BLOCKS * t + NAT_BLOCKS + 3 * j + 3)
                        copy(csb[:, (j % 2) * P:(j % 2 + 1) * P], Sb[j % 2][:, P:2 * P]).then_inc(s_c, 1)
                if k == 40:
                    act.wait_ge(s_conv, CC * t + CC)
                    act.activation(csq, conv_v, ACT.Square).then_inc(s_csq, 1)
                if k == 41:
                    act.wait_ge(s_css, t + 1)
                    act.activation(col(SSC), T1[:, 0:1], ACT.Sqrt, bias=col(EPSC), scale=1.0 / CW).then_inc(s_ssc, 1)
                for h in range(H):
                    k0 = ATT_STEP + 4 * h
                    if k == k0 + 1:
                        act.wait_ge(s_nm, H * t + h + 1)
                        act.activation(bufA[:, :], bufA[:, :], ACT.Exp, bias=nm[:, h:h + 1], scale=SCALE,
                                       accum_out=rs[:, h:h + 1]).then_inc(s_p, 1)
                    if k == k0 + 2:
                        act.wait_ge(s_pTps, 2 * H * t + 2 * h + 2)
                        if h > 0:
                            act.wait_ge(s_pv, H * t + h)
                        copy(bufB[:, 512:1024], T1[:, :]).then_inc(s_pTb, 1)
                if k == 75:
                    act.wait_ge(s_at, t + 1)
                    root(attn[:, :], CW, SSA, act_f, bufB[:, 0:CW]).then_inc(s_ssa, 1)
                if k == 82:
                    act.wait_ge(s_xm, 2 * t + 2)
                    root(x_front[:, :], D, SSM, act_f, bufB[:, :]).then_inc(s_ssm, 1)
                if k == 84:
                    for half in range(2):
                        act.wait_ge(s_hfps, 2 * t + half + 1)
                        copy(actT[:, half * 512:(half + 1) * 512], Tb[half][:, :]).then_inc(s_hfT, 1)
                for b in range(PQ_BLOCKS):
                    if k == BLOCK_STEP[IN_BLOCKS + b]:
                        act.wait_ge(s_wused, BLOCKS * t + IN_BLOCKS + b + 1)
                        if b >= 2:
                            act.wait_ge(s_s, PQ_BLOCKS * t + b - 1)
                        copy(pqT[:, (b % 2) * P:(b % 2 + 1) * P], Mb[b % 2][:, 0:P]).then_inc(s_pqT, 1)
                if k == 123:
                    act.wait_ge(s_best, t + 1)
                    act.activation(gate_front[:, :], gate_front[:, :], ACT.Exp).then_inc(s_ge, 1)

            def hand(t):
                act.wait_ge(s_xm, 2 * t + 2)
                if not first(t):
                    act.wait_ge(s_yst, 16 * t)
                copy(x_peer[:, :], x_front[:, :]).then_inc(s_handx, 1)
                act.wait_ge(s_gate, t + 1)
                copy(gate_peer[:, :], gate_front[:, :]).then_inc(s_handg, 1)
                act.wait_ge(s_handg, t + 1)

            def slot(before, k, eye, rows):
                act.wait_ge(s_dot, before + k + 1)
                act_p.link(act, act.activation(gl[:, k:k + 1], dots[:, k:k + 1], ACT.Gelu))
                act_p.link(act, copy(wk[:, k:k + 1], gl[:, k:k + 1], gate_peer[:, k:k + 1]))
                act.wait_ge(s_slot, before + k + RING - 1)
                copy(diag[:, (k % 2) * P:(k % 2) * P + rows], eye, wk[:, k:k + 1]).then_inc(s_diag, 1)

            def finish(t):
                act.wait_ge(s_x2, t + 1)
                act_y.start(t)
                root(x_peer[:, :], D, SS2, act_y, bufB[:, :]).then_inc(s_ss2, 1)

            for k in range(SLOTS):
                front(0, k)
            hand(0)
            with act.Fori(0, TILES - 1) as t:
                act_p.start(t)
                for k in range(SLOTS):
                    slot(SLOTS * t, k, ident[:, :], P)
                    front(t + 1, k)
                act_p.end()
                finish(t)
                hand(t + 1)
            act_p.start(TILES - 1)
            for k in range(SLOTS):
                slot(SLOTS * (TILES - 1), k, ident[:, :], P)
                front(S_TILE, k)
            act_p.end()
            finish(TILES - 1)
            act.wait_ge(s_xm, 2 * S_TILE + 2)
            act.wait_ge(s_yst, 16 * S_TILE)
            copy(x_peer[:, :], x_front[:, :]).then_inc(s_handx, 1)
            act.wait_ge(s_pack, 16 * 3 * PACK)
            act_p.start(TILES)
            for k in range(PSLOTS):
                slot(SLOTS * TILES, k, fold[:, :], DEC)
            finish(S_TILE)

        @block.vector
        def _(dve):
            def rstd(c_ss, c_r):
                return dve.reciprocal(col(c_r), col(c_ss))

            def rotate(x, out, n, link):
                c = rope[:, 0:HALF].unsqueeze(1).to_broadcast([P, n, HALF])
                s = rope[:, HALF:ROPE].unsqueeze(1).to_broadcast([P, n, HALF])
                r = [rtmp[:, i * H * HALF:i * H * HALF + n * HALF].rearrange("p (h c) -> p h c", h=n) for i in range(4)]
                x1, x2 = x[:, :, 0:HALF], x[:, :, HALF:ROPE]
                dve.tensor_tensor(r[0], x1, c, ALU.mult)
                dve.tensor_tensor(r[1], x2, s, ALU.mult)
                dve.tensor_tensor(r[2], x1, s, ALU.mult)
                link(dve.tensor_tensor(r[3], x2, c, ALU.mult))
                dve.tensor_tensor(out[:, :, 0:HALF], r[0], r[1], ALU.subtract)
                return dve.tensor_tensor(out[:, :, HALF:ROPE], r[2], r[3], ALU.add)

            def kv_stage(n):
                dve.wait_ge(s_ckps, n + 1)
                dve.tensor_copy(ckT, T1[:, 0:KVR]).then_inc(s_ckT, 1)

            def top16(vals, idx, src, rest, link):
                link(dve.max(vals[:, 0:8], src))
                dve.max_index(idx[:, 0:8], vals[:, 0:8], src)
                link(dve.match_replace(rest, vals[:, 0:8], src, LOWEST))
                link(dve.max(vals[:, 8:16], rest))
                return dve.max_index(idx[:, 8:16], vals[:, 8:16], rest)

            def front(t, k):
                n = S_TILE + 2 if sample(t) else t

                def link(ins):
                    dve_f.link(dve, ins)

                def link_apart(ins):
                    dve_f.link(dve, ins, wait_apart)

                if k == 1:
                    dve.wait_ge(s_ssx, t + 1)
                    rstd(SSX, RX).then_inc(s_rx, 1)
                    if first(t):
                        dve.memset(uT_v[:, :, 0:CK - 1], 0.0).then_inc(s_carry, 1)
                    elif sample(t):
                        dve.tensor_copy(convp[:, :].rearrange("p (j n) -> p j n", j=CC), uT_v[:, :, P:P + CK - 1])
                        dve.tensor_copy(uT_v[:, :, 0:CK - 1], state_v).then_inc(s_carry, 1)
                    else:
                        dve.tensor_copy(uT_v[:, :, 0:CK - 1], uT_v[:, :, P:P + CK - 1]).then_inc(s_carry, 1)
                    if sample(t):
                        dve.tensor_copy(mask[:, 0:PAST + DEC],
                                        zeros[:, 0:1].to_broadcast([P, PAST + DEC]))
                        dve.memset(mask[:, PAST + DEC:KEYS], NEG).then_inc(s_mask, 1)
                    else:
                        if first(t):
                            dve.wait_ge(s_init, 11)
                            dve.tensor_copy(mask[:, 0:P], mask_tile[:, :]).then_inc(s_mask, 1)
                        else:
                            dve.tensor_copy(mask[:, bass.ds((t - 1) * P, P)], zeros[:, :])
                            dve.tensor_copy(mask[:, bass.ds(t * P, P)], mask_tile[:, :]).then_inc(s_mask, 1)
                if k == 3:
                    if first(t):
                        dve.wait_ge(s_const, 16 * 4)
                    for half in range(2):
                        dve.wait_ge(s_hps, 2 * t + half + 1)
                        dve.tensor_tensor(actT_v[:, 4 * half:4 * half + 4, :], v3(Tb[half][:, :], 4),
                                          gain(C_GATTN + 4 * half, 4), ALU.mult).then_inc(s_hT, 1)
                if k == BLOCK_STEP[2]:
                    dve.wait_ge(s_ssz, 2 * t + 1)
                    rstd(SSQ, RQ).then_inc(s_rz, 1)
                if sample(t) and k == 7:
                    kv_stage(TILES)
                if sample(t) and k == 9:
                    kv_stage(TILES + 1)
                if k == 11:
                    dve.wait_ge(s_cqps, t + 1)
                    dve.tensor_tensor(v3(cqT, QC), v3(T0[:, 0:QR], QC), gain(C_GQ, QC), ALU.mult).then_inc(s_cqT, 1)
                if k == BLOCK_STEP[5]:
                    dve.wait_ge(s_ssz, 2 * t + 2)
                    link(rstd(SSK, RK))
                    dve.wait_ge(s_rope, 16 * (t + 1))
                    if not first(t):
                        dve.wait_ge(s_kvst, 32 * t)
                    dve.scalar_tensor_tensor(out=ckn[:, 0:KVR], in0=M1[:, 0:KVR], scalar=col(RK), in1=g_kv[:, :],
                                             op0=ALU.mult, op1=ALU.mult)
                    rotate(M1[:, KVR:KVR + ROPE].unsqueeze(1), ckn[:, KVR:KVR + ROPE].unsqueeze(1), 1,
                           link).then_inc(s_ckn, 1)
                if k == 17:
                    kv_stage(n)
                if k == 20:
                    dve.wait_ge(s_qn, 2 * t + 2)
                    pe_part = qn.rearrange("p (h c) -> p h c", h=H)[:, :, NOPE:QK]
                    rotate(pe_part, pe_part, H, link).then_inc(s_qr, 1)
                    dve.wait_ge(s_qr, t + 1)
                    dve.tensor_copy(rtmp[:, 0:1], rope[:, 0:1]).then_inc(s_ropeb, 1)
                if k == 25:
                    for half in range(2):
                        dve.wait_ge(s_qTps, 2 * t + half + 1)
                        dve.tensor_copy(qT[0:QK, half * 512:(half + 1) * 512], Mb[half][0:QK, :]).then_inc(s_qT, 1)
                for j in range(CC):
                    if k == BLOCK_STEP[NAT_BLOCKS + 3 * j + 2]:
                        dve.wait_ge(s_c, CC * t + j + 1)
                        u, o = uT_v[:, j, :], conv_v[:, j, :]
                        w = [cols[:, C_WCONV + CC * i + j:C_WCONV + CC * i + j + 1] for i in range(CK)]
                        link(dve.tensor_tensor(u[:, CK - 1:CK - 1 + P], Sb[j % 2][:, 0:P],
                                               csb[:, (j % 2) * P:(j % 2 + 1) * P], ALU.mult))
                        link(dve.tensor_scalar(o, u[:, 0:P], w[0], None, ALU.mult))
                        for i in (1, 2):
                            link(dve.scalar_tensor_tensor(out=o, in0=u[:, i:i + P], scalar=w[i], in1=o,
                                                          op0=ALU.mult, op1=ALU.add))
                        dve.tensor_tensor(o, o, Sb[j % 2][:, 2 * P:3 * P], ALU.mult).then_inc(s_conv, 1)
                if k == 40:
                    dve.wait_ge(s_conv, CC * t + CC)
                    dve.tensor_tensor(actT_v[:, 4:8, :], conv_v, gain(C_GCONV, CC), ALU.mult).then_inc(s_mixc, 1)
                if k == 41:
                    dve.wait_ge(s_ssc, t + 1)
                    rstd(SSC, RC).then_inc(s_rc, 1)
                for h in range(H):
                    k0 = ATT_STEP + 4 * h
                    if k == k0:
                        dve.wait_ge(s_sc, H * t + h + 1)
                        if h == 0:
                            wait_apart(dve, s_mask, t + 1)
                        else:
                            wait_apart(dve, s_pTps, 2 * H * t + 2 * h)
                        dve.tensor_tensor_reduce(bufA[:, :], Sps[:, :], mask[:, :], 1.0, LOWEST, ALU.add, ALU.max,
                                                 mx[:, h:h + 1]).then_inc(s_sm, 1)
                        dve.wait_ge(s_sm, H * t + h + 1)
                        dve.tensor_scalar(nm[:, h:h + 1], mx[:, h:h + 1], -SCALE, None, ALU.mult).then_inc(s_nm, 1)
                    if k == k0 + 2:
                        dve.wait_ge(s_pTps, 2 * H * t + 2 * h + 1)
                        if h > 0:
                            dve.wait_ge(s_pv, H * t + h)
                        dve.tensor_copy(bufB[:, 0:512], T0[:, :]).then_inc(s_pTa, 1)
                if k == 74:
                    dve.wait_ge(s_pv, H * t + H)
                    link(dve.reciprocal(ri[:, :], rs[:, :]))
                    dve.tensor_tensor(attn[:, :].rearrange("p (h c) -> p h c", h=H),
                                      M1[:, :].rearrange("p (h c) -> p h c", h=H),
                                      ri[:, :].unsqueeze(2).to_broadcast([P, H, VD]), ALU.mult).then_inc(s_at, 1)
                if k == 76:
                    dve.wait_ge(s_ssa, t + 1)
                    link(rstd(SSA, RA))
                    dve.wait_ge(s_aps, t + 1)
                    dve.tensor_tensor(actT_v[:, 0:4, :], v3(T0[:, :], 4), gain(C_GMLA, 4), ALU.mult).then_inc(s_mixa, 1)
                if k in (79, 81):
                    half = (k - 79) // 2
                    x = x_front[:, half * 512:(half + 1) * 512]
                    for i, c in ((0, RA), (1, RC)):
                        dve.wait_ge(s_wo, 4 * t + 2 * half + i + 1)
                        ins = dve.scalar_tensor_tensor(out=x, in0=(S0, S1, T1, M0)[2 * half + i][:, :], scalar=col(c),
                                                       in1=x, op0=ALU.mult, op1=ALU.add)
                        if i == 0:
                            link(ins)
                        else:
                            ins.then_inc(s_xm, 1)
                if k == 83:
                    dve.wait_ge(s_ssm, t + 1)
                    if first(t):
                        dve.wait_ge(s_const2, 16 * 4)
                    link(rstd(SSM, RM))
                    dve.scalar_tensor_tensor(out=hf_front[:, :], in0=x_front[:, :], scalar=col(RM), in1=g_ffn[:, :],
                                             op0=ALU.mult, op1=ALU.mult).then_inc(s_hf, 1)
                for b in range(PQ_BLOCKS):
                    if k == BLOCK_STEP[IN_BLOCKS + b] + 2:
                        wait_apart(dve, s_s, PQ_BLOCKS * t + b + 1)
                        top16(tv[:, b * TOPK:(b + 1) * TOPK], ti[:, b * TOPK:(b + 1) * TOPK],
                              Sb[b % 2][:, 0:P], s2, link_apart).then_inc(s_l1, 1)
                for h in range(PH):
                    if k == BLOCK_STEP[IN_BLOCKS + 2 * h + 1] + 3:
                        dve.wait_ge(s_l1, PQ_BLOCKS * t + 2 * h + 2)
                        va, vb = (tv[:, (2 * h + i) * TOPK:(2 * h + i + 1) * TOPK] for i in range(2))
                        dve.tensor_tensor(cand.rearrange("p (a b) -> p a b", a=TOPK),
                                          va.unsqueeze(2).to_broadcast([P, TOPK, TOPK]),
                                          vb.unsqueeze(1).to_broadcast([P, TOPK, TOPK]), ALU.add)
                        link_apart(dve.tensor_copy(tif[:, :], ti[:, 2 * h * TOPK:(2 * h + 2) * TOPK]))
                        link(top16(best[:, h * TOPK:(h + 1) * TOPK], pos, cand, cand2, link_apart))
                        dve.tensor_scalar(pab[:, 0:TOPK], pos[:, :], 4, None, ALU.logical_shift_right)
                        link(dve.tensor_scalar(pab[:, TOPK:2 * TOPK], pos[:, :], TOPK - 1, None, ALU.bitwise_and))
                        link(dve.tensor_copy(pabf[:, :], pab[:, :]))
                        for i in range(2):
                            link(dve.tensor_tensor(hot, pabf[:, i * TOPK:(i + 1) * TOPK].unsqueeze(2).to_broadcast([P, TOPK, TOPK]),
                                                   iota16[:, :].unsqueeze(1).to_broadcast([P, TOPK, TOPK]), ALU.is_equal))
                            link(dve.tensor_tensor(hot, hot, tif[:, i * TOPK:(i + 1) * TOPK].unsqueeze(1).to_broadcast([P, TOPK, TOPK]),
                                                   ALU.mult))
                            link(dve.tensor_reduce(eab[:, i * TOPK:(i + 1) * TOPK], hot, AX.X, ALU.add))
                        link(dve.scalar_tensor_tensor(out=pabf[:, 0:TOPK], in0=eab[:, 0:TOPK], scalar=float(NKEYS),
                                                      in1=eab[:, TOPK:2 * TOPK], op0=ALU.mult, op1=ALU.add))
                        if h == 0 and not first(t):
                            dve.wait_ge(s_handi, 2 * t)
                        dve.tensor_copy(idx_front[:, h * TOPK:(h + 1) * TOPK], pabf[:, 0:TOPK]).then_inc(s_idx, 1)
                if k == 123:
                    b3 = best[:, :].rearrange("p (h c) -> p h c", h=PH)
                    g3 = gate_front[:, :].rearrange("p (h c) -> p h c", h=PH)
                    if not first(t):
                        dve.wait_ge(s_handg, 1 * t)
                    dve.tensor_tensor(g3, b3, b3[:, :, 0:1].to_broadcast([P, PH, TOPK]), ALU.subtract).then_inc(s_best, 1)
                if k == 124:
                    g3 = gate_front[:, :].rearrange("p (h c) -> p h c", h=PH)
                    dve.wait_ge(s_ge, t + 1)
                    link(dve.tensor_reduce(gsum[:, 0:PH], g3, AX.X, ALU.add))
                    link(dve.reciprocal(gsum[:, PH:2 * PH], gsum[:, 0:PH]))
                    dve.tensor_tensor(g3, g3, gsum[:, PH:2 * PH].unsqueeze(2).to_broadcast([P, PH, TOPK]),
                                      ALU.mult).then_inc(s_gate, 1)

            def whole_front(t, k):
                if k == 0:
                    dve_f.start(t)
                front(t, k)
                if k == SLOTS - 1:
                    dve_f.end()

            def hand(t):
                dve.wait_ge(s_hf, t + 1)
                if not first(t):
                    dve.wait_ge(s_dot, SLOTS * t)
                dve.tensor_copy(hf_peer[:, :], hf_front[:, :]).then_inc(s_handh, 1)
                dve.wait_ge(s_handh, t + 1)

            def slot(t, k):
                dve.wait_ge(s_g[k % RING], 16 * ((SLOTS // RING) * t + k // RING + 1))
                u = ring[k % RING][:, 0:D]
                dve.tensor_tensor_reduce(u, u, hf_peer[:, :], 1.0, 0.0, ALU.mult, ALU.add,
                                         dots[:, k:k + 1]).then_inc(s_dot, 1)

            def finish(t):
                dve_y.start(t)
                dve.wait_ge(s_slot, RING + SLOTS * (t + 1) if not sample(t) else RING + SLOTS * TILES + PSLOTS)
                dve.wait_ge(s_handx, t + 1)
                rows = slice(0, DEC if sample(t) else P)
                dve.tensor_tensor(x_peer[rows, :], x_peer[rows, :], acc[rows, :], ALU.add).then_inc(s_x2, 1)
                dve.wait_ge(s_ss2, t + 1)

                def link(ins):
                    dve_y.link(dve, ins)

                link(rstd(SS2, R2))
                link(dve.scalar_tensor_tensor(out=x_peer[rows, :], in0=x_peer[rows, :], scalar=st[rows, R2:R2 + 1],
                                              in1=g_fin[rows, :], op0=ALU.mult, op1=ALU.mult))
                dve.sem_inc(s_y, 1)
                dve_y.end()

            for k in range(SLOTS):
                whole_front(0, k)
            for q in range(PACK):
                rows = slice(q * DEC, (q + 1) * DEC)
                dve.tensor_copy(fold[rows, :], ident[rows, rows]).then_inc(s_fold, 1)
            hand(0)
            with dve.Fori(0, TILES - 1) as t:
                for k in range(SLOTS):
                    slot(t, k)
                    whole_front(t + 1, k)
                finish(t)
                hand(t + 1)
            for k in range(SLOTS):
                slot(TILES - 1, k)
                whole_front(S_TILE, k)
            finish(TILES - 1)
            dve.wait_ge(s_pack, 16 * 3 * PACK)
            for k in range(PSLOTS):
                slot(TILES, k)
            finish(S_TILE)


def blocks(w):
    k, n = w.shape
    return w.reshape(k // P, P, n // P, P).transpose(2, 1, 0, 3).reshape(n // P, P, -1)


def rows(w):
    k, n = w.shape
    return w.reshape(k // P, P, n).transpose(1, 0, 2).reshape(P, -1)


def rope_table():
    at = np.concatenate([np.arange(SEQ), PAST + np.arange(P)]).astype(np.float32)
    freqs = np.float32(10000.0) ** (-np.arange(HALF, dtype=np.float32) / HALF)
    ang = at[:, None] * freqs[None, :].astype(np.float32)
    return np.concatenate([np.cos(ang), np.sin(ang)], axis=1).astype(np.float32)


def kernel(**inputs):
    import concourse.bacc as bacc
    from concourse.bass_utils import run_bass_kernel_spmd

    v = {n: np.asarray(x) for n, x in inputs.items()}
    w_in = v["w_in"][0]
    u0, b0, c0 = NATW, NATW + CW, NATW + 2 * CW
    order = [w_in[:, i * P:(i + 1) * P] for i in range(NAT_BLOCKS - 1)]
    for j in range(CC):
        order += [w_in[:, o + j * P:o + (j + 1) * P] for o in (u0, c0, b0)]
    col = lambda g: g.reshape(-1, P).T
    arrays = {
        "x_p": v["x_prompt"][0],
        "x_s": v["x_sample"][0],
        "c_kv": v["cache_kv_latent"][0, 0],
        "c_pe": v["cache_k_rope"][0, 0],
        "rope": rope_table(),
        "w_str": np.concatenate([blocks(np.concatenate(order, axis=1)), blocks(v["w_peer_q"][0])]),
        "w_nar": rows(w_in[:, NATW - ROPE:NATW]),
        "w_uq": rows(v["w_uq"][0]),
        "w_ukv": rows(v["w_ukv"][0]),
        "w_out": rows(v["w_out"][0]),
        "keysT": v["peer_keys"][0].transpose(3, 0, 1, 2).reshape(P, -1),
        "g_ffn": v["g_ffn_norm"][0],
        "g_fin": v["g_final"],
        "g_kv": v["g_kv"][0],
        "cols": np.concatenate([col(v["g_attn_norm"][0]), col(v["g_q"][0]), col(v["g_mla_out"][0]),
                                col(v["g_conv_out"][0]), *[col(w) for w in v["w_conv"][0]],
                                v["state_conv"][0, 0].reshape(CK - 1, CC, P).transpose(2, 1, 0).reshape(P, -1)],
                               axis=1),
        "uv": np.concatenate([v["peer_u"][0], v["peer_v"][0]], axis=1),
    }
    outs = {
        "o_y_p": (SEQ, D), "o_y_s": (DEC, D), "o_kv_p": (SEQ, KVR), "o_pe_p": (SEQ, ROPE),
        "o_kv_s": (DEC, KVR), "o_pe_s": (DEC, ROPE), "o_cv_p": (P, CC * (CK - 1)), "o_cv_s": (P, CC * (CK - 1)),
    }
    nc = bacc.Bacc("TRN2", target_bir_lowering=False, num_devices=1)
    arrays = {n: np.ascontiguousarray(x) for n, x in arrays.items()}
    a = {n: nc.dram_tensor(f"in_{n}", x.shape, F32, kind="ExternalInput").ap() for n, x in arrays.items()}
    a |= {n: nc.dram_tensor(n, s, F32, kind="ExternalOutput").ap() for n, s in outs.items()}
    build(nc, a)
    r = run_bass_kernel_spmd(nc, [{f"in_{n}": x for n, x in arrays.items()}], core_ids=[0]).results[0]
    conv = lambda x: x.reshape(P, CC, CK - 1).transpose(2, 1, 0).reshape(1, 1, CK - 1, CW)
    return (r["o_y_p"].reshape(1, SEQ, D), r["o_y_s"].reshape(1, DEC, D), r["o_kv_p"].reshape(1, 1, SEQ, KVR),
            r["o_pe_p"].reshape(1, 1, SEQ, ROPE), conv(r["o_cv_p"]), r["o_kv_s"].reshape(1, 1, DEC, KVR),
            r["o_pe_s"].reshape(1, 1, DEC, ROPE), conv(r["o_cv_s"]))
```

```python
from contextlib import ExitStack

import numpy as np
import concourse.bass as bass
from concourse import mybir

F32 = mybir.dt.float32
U32 = mybir.dt.uint32
ALU = mybir.AluOpType
ACT = mybir.ActivationFunctionType
AX = mybir.AxisListType

P = 128
D = 1024
KC = D // P
SEQ, DEC, PAST = 1024, 32, 256
TILES = SEQ // P
S_TILE = TILES
CHUNK = 64
EPS = 1e-6
NEG = -1e30
LOWEST = -3.0e38
H, NOPE, ROPE, VD = 8, 64, 32, 64
QK = NOPE + ROPE
HALF = ROPE // 2
SCALE = float(QK) ** -0.5
QR, KVR, CW, CK = 384, 256, 512, 3
QC, CC = QR // P, CW // P
NATW = QR + KVR + ROPE
NKEYS, TOPK, PH = 128, 16, 8
NEXP = NKEYS * NKEYS
SLOTS = PH * TOPK
KEYS = SEQ
KB = KEYS // P

NAT_BLOCKS = 6
IN_BLOCKS = NAT_BLOCKS + 3 * CC
PQ_BLOCKS = 2 * PH
BLOCKS = IN_BLOCKS + PQ_BLOCKS
WBUF = 2
RING = 4
LEAD = 2 * RING
PACK = P // DEC
PSLOTS = SLOTS // PACK

BLOCK_STEP = [4 + 4 * b // 3 for b in range(IN_BLOCKS)] + [77 + 5 * b // 2 for b in range(PQ_BLOCKS)]
ATT_STEP = 29
LAG = 2
PAST_STEPS = {6: ((0, 0),), 8: ((0, 1), (0, 2)), 9: ((1, 0),), 11: ((1, 1),), 13: ((1, 2),)}
ACT_FRONT = 5
DVE_FRONT = 186

C_GATTN, C_GQ, C_GMLA, C_GCONV, C_WCONV, C_STATE = 0, 8, 11, 15, 19, 31
NCOLS = 39


def first(t):
    return isinstance(t, int) and t == 0


def key_blocks(t):
    return 1 if first(t) else PAST // P + 1 if sample(t) else KB


def sample(t):
    return isinstance(t, int) and t == S_TILE


class Count:

    def __init__(self, sem, per):
        self.sem, self.per = sem, per

    def start(self, t):
        self.t, self.n = t, 0

    def link(self, eng, ins, wait=None):
        self.n += 1
        ins.then_inc(self.sem, 1)
        (wait or type(eng).wait_ge)(eng, self.sem, self.per * self.t + self.n)

    def end(self):
        assert self.n == self.per, (self.n, self.per)


def build(nc, a):
    with ExitStack() as ctx:
        def sb(name, cols, dt=F32):
            return ctx.enter_context(nc.sbuf_tensor(name, [P, cols], dt))

        def psum(name):
            return ctx.enter_context(nc.psum_tensor(name, [P, 512], F32))

        def sem(name):
            return ctx.enter_context(nc.semaphore(name))

        w_out = sb("w_out_sb", KC * D)
        w_uq = sb("w_uq_sb", QC * H * QK)
        w_ukv = sb("w_ukv_sb", 2 * H * (NOPE + VD))
        keysT = sb("keysT_sb", PQ_BLOCKS * NKEYS)
        g_ffn = sb("g_ffn_sb", D)
        g_fin = sb("g_fin_sb", D)
        g_kv = sb("g_kv_sb", KVR)
        cols = sb("cols_sb", NCOLS)
        kT = sb("kT", H * KEYS)
        vv = sb("vv", KB * H * VD)
        wst = [sb(f"wst{i}", KC * P) for i in range(WBUF)]
        ring = [sb(f"ring{i}", 2 * D) for i in range(RING)]
        x_front = sb("x_front", D)
        x_peer = sb("x_peer", D)
        hf_front = sb("hf_front", D)
        hf_peer = sb("hf_peer", D)
        idx_front = sb("idx_front", SLOTS, U32)
        idx_peer = sb("idx_peer", SLOTS, U32)
        idx_lead = sb("idx_lead", LEAD, U32)
        idx_pack = sb("idx_pack", PSLOTS, U32)
        gate_pack = sb("gate_pack", PSLOTS)
        y_buf = sb("y_buf", D)
        gate_front = sb("gate_front", SLOTS)
        gate_peer = sb("gate_peer", SLOTS)
        rope = sb("rope", ROPE)
        actT = sb("actT", KC * P)
        ckn = sb("ckn", KVR + ROPE)
        qT = sb("qT", H * P)
        cqT = qT[:, 0:QR]
        ckT = qT[:, QR:QR + KVR]
        uT = sb("uT", CC * (P + CK - 1))
        convT = sb("convT", CW)
        attn = convT
        convp = sb("convp", CC * (CK - 1))
        csb = sb("csb", 2 * P)
        mask = sb("mask", KEYS)
        mask_tile = sb("mask_tile", P)
        zeros = sb("zeros", P)
        ident = sb("ident", P)
        fold = sb("fold", DEC)
        ones = sb("ones", 1)
        bufA = sb("bufA", D)
        bufB = sb("bufB", D)
        diag = sb("diag", 2 * P)
        rtmp = bufA[:, D - 4 * H * HALF:D]
        tv = sb("tv", PQ_BLOCKS * TOPK)
        ti = sb("ti", PQ_BLOCKS * TOPK, U32)
        tif = sb("tif", 2 * TOPK)
        best = sb("best", SLOTS)
        pos = sb("pos", TOPK, U32)
        pab = sb("pab", 2 * TOPK, U32)
        pabf = sb("pabf", 2 * TOPK)
        eab = sb("eab", 2 * TOPK)
        iota16 = sb("iota16", TOPK)
        gsum = sb("gsum", 2 * PH)
        dots = sb("dots", SLOTS)
        gl = sb("gl", SLOTS)
        wk = sb("wk", SLOTS)
        st = sb("st", 24)
        mx = sb("mx", H)
        nm = sb("nm", H)
        rs = sb("rs", H)
        ri = sb("ri", H)

        acc = ctx.enter_context(nc.psum_tensor("acc", [P, 2 * 512], F32))
        Sps = ctx.enter_context(nc.psum_tensor("Sps", [P, 2 * 512], F32))
        S0, S1 = Sps[:, 0:512], Sps[:, 512:1024]
        T0, T1, M0, M1 = [psum(n) for n in ("T0", "T1", "M0", "M1")]

        s_passed = {e: sem(f"s_passed_{e}") for e in ("pool", "dve")}

        def wait_apart(eng, s, value):
            eng.wait_ge(s, value)
            eng.sem_inc(s_passed["pool" if eng is nc.gpsimd else "dve"], 1)

        s_const = sem("s_const")
        s_const2 = sem("s_const2")
        s_x = sem("s_x_loaded")
        s_rope = sem("s_rope_loaded")
        s_w = [sem(f"s_w_loaded{i}") for i in range(WBUF)]
        s_wused = sem("s_w_used")
        s_past = sem("s_past_loaded")
        s_kvst = sem("s_kv_stored")
        s_cpst = sem("s_conv_stored")
        s_yst = sem("s_y_stored")
        s_g = [sem(f"s_gathered{i}") for i in range(RING)]
        s_init = sem("s_init")
        s_fold = sem("s_fold")
        s_ropeb = sem("s_rope_used")
        s_ssx = sem("s_ssx")
        s_rx = sem("s_rx")
        s_h = sem("s_h")
        s_hps = sem("s_h_turned")
        s_hT = sem("s_hT")
        s_ssz = sem("s_ssz")
        s_rz = sem("s_rz")
        s_cqn = sem("s_cqn")
        s_ckn = sem("s_ckn")
        s_cqps = sem("s_cq_turned")
        s_cqT = sem("s_cqT")
        s_ckps = sem("s_ck_turned")
        s_ckT = sem("s_ckT")
        s_kpe = sem("s_kpe")
        s_kvps = sem("s_kv_ps")
        s_kv = sem("s_kv_kept")
        s_qps = sem("s_q_ps")
        s_qn = sem("s_qn")
        s_qr = sem("s_q_rotated")
        s_qTps = sem("s_q_turned")
        s_qT = sem("s_qT")
        s_ucb = sem("s_ucb")
        s_c = sem("s_c")
        s_conv = sem("s_conv")
        s_carry = sem("s_carry")
        s_csq = sem("s_csq")
        s_mixc = sem("s_mixc")
        s_css = sem("s_css")
        s_ssc = sem("s_ssc")
        s_rc = sem("s_rc")
        s_mask = sem("s_mask")
        s_sc = sem("s_scores")
        s_sm = sem("s_masked")
        s_nm = sem("s_negmax")
        s_p = sem("s_probs")
        s_pTps = sem("s_p_turned")
        s_pTa = sem("s_pT_low")
        s_pTb = sem("s_pT_high")
        s_pv = sem("s_pv")
        s_at = sem("s_attn")
        s_ssa = sem("s_ssa")
        s_aps = sem("s_attn_turned")
        s_mixa = sem("s_mixa")
        s_wo = sem("s_wo")
        s_xm = sem("s_xmid")
        s_ssm = sem("s_ssm")
        s_hf = sem("s_hf")
        s_hfps = sem("s_hf_turned")
        s_hfT = sem("s_hfT")
        s_pq = sem("s_pq")
        s_pqT = sem("s_pqT")
        s_s = sem("s_keyscores")
        s_l1 = sem("s_level1")
        s_idx = sem("s_idx")
        s_best = sem("s_best")
        s_ge = sem("s_gate_exp")
        s_gate = sem("s_gate")
        s_handx = sem("s_hand_x")
        s_handh = sem("s_hand_hf")
        s_handg = sem("s_hand_gate")
        s_handi = sem("s_hand_idx")
        s_pack = sem("s_packed")
        s_dot = sem("s_dot")
        s_diag = sem("s_diag")
        s_slot = sem("s_slot_done")
        s_x2 = sem("s_x2")
        s_ss2 = sem("s_ss2")
        s_y = sem("s_y")
        dve_f = Count(sem("s_dve_front"), DVE_FRONT)
        act_f = Count(sem("s_act_front"), ACT_FRONT)
        act_y = Count(sem("s_act_final"), 1)
        act_p = Count(sem("s_act_peer"), 2 * SLOTS)
        dve_y = Count(sem("s_dve_final"), 2)

        w_out_v = w_out[:, :].rearrange("p (k n) -> p k n", k=KC)
        w_uq_v = w_uq[:, :].rearrange("p (k n) -> p k n", k=QC)
        w_ukv_v = w_ukv[:, :].rearrange("p (k h c) -> p k h c", k=2, h=H)
        keysT_v = keysT[:, :].rearrange("p (b n) -> p b n", b=PQ_BLOCKS)
        wst_v = [w[:, :].rearrange("p (k n) -> p k n", k=KC) for w in wst]
        kT_v = kT[:, :].rearrange("p (h k) -> p h k", h=H)
        actT_v = actT[:, :].rearrange("p (k n) -> p k n", k=KC)
        uT_v = uT[:, :].rearrange("p (j n) -> p j n", j=CC)
        conv_v = convT[:, :].rearrange("p (j n) -> p j n", j=CC)
        state_v = cols[:, C_STATE:C_STATE + 8].rearrange("p (j n) -> p j n", j=CC)
        past = bufA[:, 448:1024].rearrange("p (b n) -> p b n", b=2)
        csq = bufB[:, 0:CW].rearrange("p (j n) -> p j n", j=CC)
        hnat = bufA
        hf_pack = bufA
        cqn = bufA[:, 0:QR]
        qn = bufB[:, 0:H * QK]
        pqT = bufB[:, 0:2 * P]
        s2 = bufA[:, 0:128]
        cand = bufA[:, 128:384]
        cand2 = bufA[:, 384:640]
        hot = bufA[:, 640:896].rearrange("p (k c) -> p k c", c=TOPK)
        Sb = [S0, S1]
        Tb = [T0, T1]
        Mb = [M0, M1]
        SSX, RX, SSQ, RQ, SSK, RK, RC, SSA, RA, SSM, RM, SS2, R2, SSC, EPSC = range(15)

        def col(c):
            return st[:, c:c + 1]

        def gain(c, n):
            return cols[:, c:c + n].unsqueeze(2).to_broadcast([P, n, P])

        def v3(ap, n):
            return ap.rearrange("p (k n) -> p k n", k=n)

        block = ctx.enter_context(nc.Block())

        @block.sync
        def _(sp):
            def load_block(t, b):
                if b >= WBUF or not isinstance(t, int) or t > 0:
                    sp.wait_ge(s_wused, BLOCKS * t + b - WBUF + 1)
                if b == NAT_BLOCKS - 1:
                    sp.dma_start(wst_v[b % WBUF][:, :, 0:ROPE],
                                 a["w_nar"].rearrange("p (k n) -> p k n", k=KC)).then_inc(s_w[b % WBUF], 16)
                else:
                    sp.dma_start(wst[b % WBUF][:, :], a["w_str"][b - (b >= NAT_BLOCKS)]).then_inc(s_w[b % WBUF], 16)

            def front(t, k):
                if k == 0:
                    if not first(t):
                        sp.wait_ge(s_handx, t)
                    if sample(t):
                        sp.dma_start(x_front[0:DEC, :], a["x_s"]).then_inc(s_x, 16)
                    else:
                        sp.dma_start(x_front[:, :], a["x_p"][bass.ds(t * P, P), :]).then_inc(s_x, 16)
                    if not first(t):
                        sp.wait_ge(s_ropeb, 1 * t)
                    sp.dma_start(rope[:, :], a["rope"][bass.ds(t * P, P), :]).then_inc(s_rope, 16)
                for b in range(BLOCKS):
                    if max(0, BLOCK_STEP[b] - 4) == k:
                        load_block(t, b)
                if sample(t) and k == 4:
                    sp.wait_ge(s_hps, 2 * t + 2)
                    sp.dma_start(past[:, :, 0:KVR], a["c_kv"].rearrange("(b p) n -> p b n", p=P)).then_inc(s_past, 16)
                    sp.dma_start(past[:, :, KVR:KVR + ROPE],
                                 a["c_pe"].rearrange("(b p) n -> p b n", p=P)).then_inc(s_past, 16)
                if k == 22:
                    sp.wait_ge(s_ckn, t + 1)
                    if sample(t):
                        sp.dma_start(a["o_kv_s"], ckn[0:DEC, 0:KVR]).then_inc(s_kvst, 16)
                        sp.dma_start(a["o_pe_s"], ckn[0:DEC, KVR:KVR + ROPE]).then_inc(s_kvst, 16)
                    else:
                        sp.dma_start(a["o_kv_p"][bass.ds(t * P, P), :], ckn[:, 0:KVR]).then_inc(s_kvst, 16)
                        sp.dma_start(a["o_pe_p"][bass.ds(t * P, P), :], ckn[:, KVR:KVR + ROPE]).then_inc(s_kvst, 16)
                if k == 40 and sample(t):
                    sp.wait_ge(s_carry, S_TILE + 1)
                    sp.dma_start(a["o_cv_p"], convp[:, :]).then_inc(s_cpst, 16)
                    sp.wait_ge(s_conv, CC * (t + 1))
                    sp.dma_start(a["o_cv_s"].rearrange("p (j n) -> p j n", j=CC),
                                 uT_v[:, :, DEC:DEC + CK - 1]).then_inc(s_cpst, 16)

            def store_y(t):
                sp.wait_ge(s_y, t + 1)
                if sample(t):
                    sp.dma_start(a["o_y_s"], y_buf[0:DEC, :]).then_inc(s_yst, 16)
                else:
                    sp.dma_start(a["o_y_p"][bass.ds(t * P, P), :], y_buf[:, :]).then_inc(s_yst, 16)

            sp.dma_start(cols[:, :], a["cols"]).then_inc(s_const, 16)
            front(0, 0)
            for dst, src in ((g_kv, a["g_kv"].partition_broadcast(P)), (w_uq, a["w_uq"]), (w_ukv, a["w_ukv"])):
                sp.dma_start(dst[:, :], src).then_inc(s_const, 16)
            for k in range(1, SLOTS):
                front(0, k)
                if k == 14:
                    for dst, src in ((w_out, a["w_out"]), (g_ffn, a["g_ffn"].partition_broadcast(P)),
                                     (keysT, a["keysT"]), (g_fin, a["g_fin"].partition_broadcast(P))):
                        sp.dma_start(dst[:, :], src).then_inc(s_const2, 16)
            for k in range(SLOTS):
                front(1, k)
            with sp.Fori(1, TILES - 1) as t:
                for k in range(SLOTS):
                    front(t + 1, k)
                    if k == 8:
                        store_y(t - 1)
            for k in range(SLOTS):
                front(S_TILE, k)
                if k == 8:
                    store_y(TILES - 2)
            sp.wait_ge(s_idx, PH * (S_TILE + 1))
            sp.wait_ge(s_gate, S_TILE + 1)
            for q in range(PACK):
                group = slice(q * DEC, (q + 1) * DEC)
                part = slice(q * PSLOTS, (q + 1) * PSLOTS)
                sp.dma_start(idx_pack[group, :], idx_front[0:DEC, part]).then_inc(s_pack, 16)
                sp.dma_start(gate_pack[group, :], gate_front[0:DEC, part]).then_inc(s_pack, 16)
                sp.dma_start(hf_pack[group, :], hf_front[0:DEC, :]).then_inc(s_pack, 16)
            store_y(TILES - 1)
            store_y(S_TILE)
            sp.wait_ge(s_yst, 16 * (S_TILE + 1))
            sp.wait_ge(s_kvst, 32 * (S_TILE + 1))
            sp.wait_ge(s_cpst, 32)

        @block.gpsimd
        def _(pool):
            pool.memset(ident[:, :], 0.0).then_inc(s_init, 1)
            pool.memset(mask_tile[:, :], 0.0).then_inc(s_init, 1)
            pool.memset(ones[:, :], 1.0).then_inc(s_init, 1)
            pool.memset(zeros[:, :], 0.0).then_inc(s_init, 1)
            pool.iota(iota16[:, :], pattern=[[1, TOPK]], base=0, channel_multiplier=0,
                      allow_small_or_imprecise_dtypes=True).then_inc(s_init, 1)
            pool.wait_ge(s_init, 5)
            pool.affine_select(out=ident[:, :], in_=ident[:, :], compare_op=ALU.not_equal, fill=1.0, base=0,
                               pattern=[[-1, P]], channel_multiplier=1).then_inc(s_init, 1)
            pool.memset(mask_tile[0:CHUNK, CHUNK:P], NEG).then_inc(s_init, 1)
            pool.sem_inc(s_slot, RING)
            pool.memset(col(EPSC), EPS).then_inc(s_init, 1)
            pool.memset(kT[:, :], 0.0).then_inc(s_init, 1)
            pool.memset(vv[:, :], 0.0).then_inc(s_init, 1)
            pool.memset(mask[:, :], NEG).then_inc(s_init, 1)

            def gather(tile, k, before):
                wait_apart(pool, s_slot, before + k + 1)
                src = idx_pack if sample(tile) else idx_lead if k < LEAD else idx_peer
                pool.indirect_dma_start(ring[k % RING][:, :], None, a["uv"],
                                        bass.IndirectOffsetOnAxis(ap=src[:, k:k + 1], axis=0)
                                        ).then_inc(s_g[k % RING], 16)
                if sample(tile):
                    return
                if k == RING - 1:
                    wait_apart(pool, s_idx, PH * (tile + 1))
                    pool.tensor_copy(idx_peer[:, LEAD:SLOTS], idx_front[:, LEAD:SLOTS]).then_inc(s_handi, 1)
                if k == LEAD - 1:
                    wait_apart(pool, s_handi, 2 * tile + 2)

            def hand(t):
                wait_apart(pool, s_idx, PH * t + 1)
                pool.tensor_copy(idx_lead[:, :], idx_front[:, 0:LEAD]).then_inc(s_handi, 1)
                wait_apart(pool, s_handi, 2 * t + 1)

            def body(t):
                hand(t)
                for k in range(SLOTS):
                    gather(t, k, SLOTS * t)

            body(0)
            with pool.Fori(1, TILES - 1) as t:
                body(t)
            body(TILES - 1)
            pool.wait_ge(s_pack, 16 * 3 * PACK)
            for k in range(PSLOTS):
                gather(S_TILE, k, SLOTS * TILES)

        @block.tensor
        def _(pe):
            def turn(dst, src, rows=P):
                return pe.transpose(dst, src, ident[:, :])

            def w_ready(t, b):
                pe.wait_ge(s_w[b % WBUF], 16 * ((BLOCKS // WBUF) * t + b // WBUF + 1))

            def in_block(t, b):
                w_ready(t, b)
                w = wst_v[b % WBUF]
                if b < NAT_BLOCKS:
                    n = ROPE if b == NAT_BLOCKS - 1 else P
                    bank = Mb[b // QC]
                    at = (b % QC) * P
                    if b % QC == 0 and not first(t):
                        pe.wait_ge(s_pqT, PQ_BLOCKS * t)
                    for c in range(KC):
                        mm = pe.matmul(bank[:, at:at + n], actT_v[:, c, :], w[:, c, 0:n],
                                       start=(c == 0), stop=(c == KC - 1))
                    mm.then_inc(s_wused, 1)
                else:
                    j, part = divmod(b - NAT_BLOCKS, 3)
                    bank = Sb[j % 2]
                    if part == 0:
                        if j >= 2:
                            pe.wait_ge(s_conv, CC * t + j - 1)
                        elif not first(t):
                            pe.wait_ge(s_l1, PQ_BLOCKS * t)
                            if sample(t):
                                pe.wait_ge(s_kv, 3 * (TILES + 1) + 2)
                    for c in range(KC):
                        mm = pe.matmul(bank[:, part * P:(part + 1) * P], w[:, c, :], actT_v[:, c, :],
                                       start=(c == 0), stop=(c == KC - 1))
                    mm.then_inc(s_wused, 1)

            def kv_stage(n, src, k):
                if k == 0:
                    if not first(n):
                        pe.wait_ge(s_kv, 3 * n)
                    for i, (lo, hi) in enumerate(((0, P), (P, 2 * P), (KVR + ROPE - QK, KVR + ROPE))):
                        mm = turn(T1[0:hi - lo, i * P:(i + 1) * P], src[:, lo:hi])
                    mm.then_inc(s_ckps, 1)
                if k == 1:
                    pe.wait_ge(s_ckT, n + 1)
                    pe.wait_ge(s_kpe, n + 1)
                    banks = Sb if src is not ckn else Tb
                    for half in range(2):
                        for h in range(4):
                            for c in range(2):
                                mm = pe.matmul(banks[half][0:NOPE, h * P:(h + 1) * P], w_ukv_v[:, c, 4 * half + h, 0:NOPE],
                                               ckT[:, c * P:(c + 1) * P], start=(c == 0), stop=(c == 1))
                        mm.then_inc(s_kvps, 1)
                if k == 2:
                    if src is ckn:
                        pe.wait_ge(s_kv, 3 * n + 1)
                    elif n == TILES + 1:
                        pe.wait_ge(s_cqT, S_TILE + 1)
                    for c in range(2):
                        mm = pe.matmul(T0[:, :].rearrange("p (h c) -> p h c", h=H), ckT[:, c * P:(c + 1) * P],
                                       w_ukv_v[:, c, :, NOPE:NOPE + VD], start=(c == 0), stop=(c == 1))
                    mm.then_inc(s_kvps, 1)

            def front(t, k):
                n = S_TILE + 2 if sample(t) else t
                if k == 3:
                    pe.wait_ge(s_h, t + 1)
                    if first(t):
                        pe.wait_ge(s_init, 11)
                        pe.wait_ge(s_const, 16 * 4)
                    for c in range(KC):
                        mm = turn(Tb[c // 4][:, (c % 4) * P:(c % 4 + 1) * P], hnat[:, c * P:(c + 1) * P])
                        if c % 4 == 3:
                            mm.then_inc(s_hps, 1)
                if k == BLOCK_STEP[0]:
                    pe.wait_ge(s_hT, 2 * t + 2)
                if sample(t):
                    if k == 6:
                        pe.wait_ge(s_past, 32)
                    for b, part in PAST_STEPS.get(k, ()):
                        kv_stage(TILES + b, past[:, b, :], part)
                if k == 10:
                    pe.wait_ge(s_cqn, t + 1)
                    if sample(t):
                        pe.wait_ge(s_kv, 3 * TILES + 3)
                    for c in range(QC):
                        mm = turn(T0[:, c * P:(c + 1) * P], cqn[:, c * P:(c + 1) * P])
                    mm.then_inc(s_cqps, 1)
                if k == 14:
                    pe.wait_ge(s_ckn, t + 1)
                    kv_stage(n, ckn, 0)
                if k in (13, 15):
                    half = (k - 13) // 2
                    if half == 0:
                        pe.wait_ge(s_cqT, t + 1)
                    else:
                        pe.wait_ge(s_ckn, t + 1)
                    for c in range(QC):
                        mm = pe.matmul(Mb[half][:, 0:QR], cqT[:, c * P:(c + 1) * P],
                                       w_uq_v[:, c, half * QR:(half + 1) * QR], start=(c == 0), stop=(c == QC - 1))
                    mm.then_inc(s_qps, 1)
                if k == 17:
                    kv_stage(n, ckn, 1)
                if k == 20:
                    kv_stage(n, ckn, 2)
                if k == 21:
                    pe.wait_ge(s_qr, t + 1)
                    for h in range(H):
                        mm = turn(Mb[h // 4][0:QK, (h % 4) * P:(h % 4 + 1) * P], qn[:, h * QK:(h + 1) * QK])
                        if h % 4 == 3:
                            mm.then_inc(s_qTps, 1)
                for b in range(IN_BLOCKS):
                    if BLOCK_STEP[b] == k:
                        in_block(t, b)
                if k == 30:
                    pe.wait_ge(s_csq, t + 1)
                    pe.wait_ge(s_kv, 3 * n + 3)
                    for j in range(CC):
                        mm = pe.matmul(T1[:, 0:1], csq[:, j, :], ones[:, 0:1], start=(j == 0), stop=(j == CC - 1))
                    mm.then_inc(s_css, 1)
                nb = key_blocks(t)
                for h in range(H):
                    k0 = ATT_STEP + 4 * h
                    if k == k0:
                        if h == 0:
                            pe.wait_ge(s_qT, 2 * t + 2)
                            pe.wait_ge(s_conv, CC * t + CC)
                        else:
                            pe.wait_ge(s_sm, H * t + h)
                        for lo in range(0, nb * P, 512):
                            n_keys = min(512, nb * P - lo)
                            mm = pe.matmul(Sps[:, lo:lo + n_keys], qT[0:QK, h * P:(h + 1) * P],
                                           kT_v[0:QK, h, lo:lo + n_keys], start=True, stop=True)
                        mm.then_inc(s_sc, 1)
                    if k == k0 + 3:
                        pe.wait_ge(s_p, H * t + h + 1)
                        if h == 0:
                            pe.wait_ge(s_rc, t + 1)
                        else:
                            pe.wait_ge(s_pTa, H * t + h)
                            pe.wait_ge(s_pTb, H * t + h)
                        for c in range(nb):
                            mm = turn(Tb[c // 4][:, (c % 4) * P:(c % 4 + 1) * P], bufA[:, c * P:(c + 1) * P])
                            if c == nb - 1 or c == 3:
                                mm.then_inc(s_pTps, 1 if nb > 4 else 2)
                    if k == k0 + 5:
                        pe.wait_ge(s_pTa, H * t + h + 1)
                        pe.wait_ge(s_pTb, H * t + h + 1)
                        for c in range(nb):
                            mm = pe.matmul(M1[:, h * VD:(h + 1) * VD], bufB[:, c * P:(c + 1) * P],
                                           vv[:, (c * H + h) * VD:(c * H + h + 1) * VD],
                                           start=(c == 0), stop=(c == nb - 1))
                        mm.then_inc(s_pv, 1)
                if k == 65:
                    pe.wait_ge(s_at, t + 1)
                    for c in range(4):
                        mm = turn(T0[:, c * P:(c + 1) * P], attn[:, c * P:(c + 1) * P])
                    mm.then_inc(s_aps, 1)
                if 67 <= k < 71:
                    i = k - 67
                    if i == 0:
                        pe.wait_ge(s_mixa, t + 1)
                        if first(t):
                            pe.wait_ge(s_const2, 16 * 4)
                        pe.wait_ge(s_mixc, t + 1)
                        pe.wait_ge(s_sm, H * t + H)
                    bank = (S0, S1, T1, M0)[i]
                    for c in range(4):
                        mm = pe.matmul(bank[:, :], actT_v[:, 4 * (i % 2) + c, :],
                                       w_out_v[:, 4 * (i % 2) + c, (i // 2) * 512:(i // 2 + 1) * 512],
                                       start=(c == 0), stop=(c == 3))
                    mm.then_inc(s_wo, 1)
                if k == 75:
                    pe.wait_ge(s_hf, t + 1)
                    for c in range(KC):
                        mm = turn(Tb[c // 4][:, (c % 4) * P:(c % 4 + 1) * P], hf_front[:, c * P:(c + 1) * P])
                        if c % 4 == 3:
                            mm.then_inc(s_hfps, 1)
                for b in range(PQ_BLOCKS):
                    if k == BLOCK_STEP[IN_BLOCKS + b]:
                        if b == 0:
                            pe.wait_ge(s_hfT, 2 * t + 2)
                        if b >= 2:
                            pe.wait_ge(s_pqT, PQ_BLOCKS * t + b - 1)
                        w_ready(t, IN_BLOCKS + b)
                        w = wst_v[(IN_BLOCKS + b) % WBUF]
                        for c in range(KC):
                            mm = pe.matmul(Mb[b % 2][:, 0:P], w[:, c, :], actT_v[:, c, :],
                                           start=(c == 0), stop=(c == KC - 1))
                        mm.then_inc(s_wused, 1)
                    if k == BLOCK_STEP[IN_BLOCKS + b] + 3:
                        pe.wait_ge(s_pqT, PQ_BLOCKS * t + b + 1)
                        if b >= 2:
                            pe.wait_ge(s_l1, PQ_BLOCKS * t + b - 1)
                        pe.matmul(Sb[b % 2][:, 0:P], pqT[:, (b % 2) * P:(b % 2 + 1) * P],
                                  keysT_v[:, b, :], start=True, stop=True).then_inc(s_s, 1)

            def slot(before, k, n, rows):
                pe.wait_ge(s_diag, before + k + 1)
                for half in range(2):
                    mm = pe.matmul(acc[0:rows, half * 512:(half + 1) * 512], diag[:, (k % 2) * P:(k % 2) * P + rows],
                                   ring[k % RING][:, D + half * 512:D + (half + 1) * 512],
                                   start=(k == 0), stop=(k == n - 1))
                mm.then_inc(s_slot, 1)

            def body(t):
                for k in range(SLOTS):
                    if k == 0 and not first(t):
                        pe.wait_ge(s_x2, 1 * t)
                    slot(SLOTS * t, k, SLOTS, P)
                    front(t + 1, k)

            for k in range(SLOTS):
                front(0, k)
            body(0)
            with pe.Fori(1, TILES - 1) as t:
                body(t)
            body(TILES - 1)
            pe.wait_ge(s_x2, TILES)
            for k in range(PSLOTS):
                slot(SLOTS * TILES, k, PSLOTS, DEC)

        @block.scalar
        def _(act):
            def copy(out, in_, scale=1.0):
                return act.activation(out, in_, ACT.Copy, scale=scale)

            def root(src, n, c, count, junk):
                count.link(act, act.activation(junk, src, ACT.Square, accum_out=col(c)))
                return act.activation(col(c), col(c), ACT.Sqrt, bias=col(EPSC), scale=1.0 / n)

            def kv_stage(n, at, k):
                if k == 0:
                    act.wait_ge(s_ckT, n + 1)
                    copy(kT_v[NOPE:QK, :, bass.ds(at * P, P)],
                         T1[NOPE:QK, 2 * P:3 * P].unsqueeze(1).to_broadcast([ROPE, H, P])).then_inc(s_kpe, 1)
                if k == 1:
                    for half in range(2):
                        act.wait_ge(s_kvps, 3 * n + half + 1)
                        banks = Sb if isinstance(n, int) and TILES <= n < TILES + 2 else Tb
                        copy(kT_v[0:NOPE, 4 * half:4 * half + 4, bass.ds(at * P, P)],
                             v3(banks[half][0:NOPE, :], 4)).then_inc(s_kv, 1)
                if k == 2:
                    act.wait_ge(s_kvps, 3 * n + 3)
                    copy(vv[:, bass.ds(at * 512, 512)], T0[:, :]).then_inc(s_kv, 1)

            def front(t, k):
                n = S_TILE + 2 if sample(t) else t
                at = PAST // P if sample(t) else t
                if k == 0:
                    act_f.start(t)
                    if first(t):
                        act.wait_ge(s_init, 11)
                if k == 1:
                    act.wait_ge(s_x, 16 * (t + 1))
                    root(x_front[:, :], D, SSX, act_f, bufB[:, :]).then_inc(s_ssx, 1)
                if k == 2:
                    act.wait_ge(s_rx, t + 1)
                    copy(hnat[:, :], x_front[:, :], col(RX)).then_inc(s_h, 1)
                if sample(t):
                    for b, part in PAST_STEPS.get(k, ()):
                        kv_stage(TILES + b, b, part)
                if k == BLOCK_STEP[2]:
                    act.wait_ge(s_wused, BLOCKS * t + 3)
                    root(M0[:, 0:QR], QR, SSQ, act_f, bufB[:, 0:QR]).then_inc(s_ssz, 1)
                if k == BLOCK_STEP[2] + 1:
                    act.wait_ge(s_rz, t + 1)
                    copy(cqn, M0[:, 0:QR], col(RQ)).then_inc(s_cqn, 1)
                if k == BLOCK_STEP[5]:
                    act.wait_ge(s_wused, BLOCKS * t + 6)
                    root(M1[:, 0:KVR], KVR, SSK, act_f, bufB[:, QR:QR + KVR]).then_inc(s_ssz, 1)
                if k == 14:
                    if first(t):
                        act.wait_ge(s_init, 11)
                    kv_stage(n, at, 0)
                if k in (13, 15):
                    half = (k - 13) // 2
                    act.wait_ge(s_qps, 2 * t + half + 1)
                    copy(qn[:, half * QR:(half + 1) * QR], Mb[half][:, 0:QR]).then_inc(s_qn, 1)
                if k == 17:
                    kv_stage(n, at, 1)
                if k == 20:
                    kv_stage(n, at, 2)
                for j in range(CC):
                    if k == BLOCK_STEP[NAT_BLOCKS + 3 * j + 2]:
                        act.wait_ge(s_wused, BLOCKS * t + NAT_BLOCKS + 3 * j + 3)
                        copy(csb[:, (j % 2) * P:(j % 2 + 1) * P], Sb[j % 2][:, P:2 * P]).then_inc(s_c, 1)
                if k == 27:
                    act.wait_ge(s_conv, CC * t + CC)
                    act.activation(csq, conv_v, ACT.Square).then_inc(s_csq, 1)
                if k == 30:
                    act.wait_ge(s_css, t + 1)
                    act.activation(col(SSC), T1[:, 0:1], ACT.Sqrt, bias=col(EPSC), scale=1.0 / CW).then_inc(s_ssc, 1)
                nk = key_blocks(t) * P
                for h in range(H):
                    k0 = ATT_STEP + 4 * h
                    if k == k0:
                        act.wait_ge(s_nm, H * t + h + 1)
                        act.activation(bufA[:, 0:nk], bufA[:, 0:nk], ACT.Exp, bias=nm[:, h:h + 1], scale=SCALE,
                                       accum_out=rs[:, h:h + 1]).then_inc(s_p, 1)
                    if k == k0 + 3 and nk <= 512:
                        act.sem_inc(s_pTb, 1)
                    elif k == k0 + 3:
                        act.wait_ge(s_pTps, 2 * H * t + 2 * h + 2)
                        if h > 0:
                            act.wait_ge(s_pv, H * t + h)
                        copy(bufB[:, 512:1024], T1[:, :]).then_inc(s_pTb, 1)
                if k == 63:
                    act.wait_ge(s_at, t + 1)
                    root(attn[:, :], CW, SSA, act_f, bufB[:, 0:CW]).then_inc(s_ssa, 1)
                if k == 71:
                    act.wait_ge(s_xm, 2 * t + 2)
                    root(x_front[:, :], D, SSM, act_f, bufB[:, :]).then_inc(s_ssm, 1)
                if k == 75:
                    for half in range(2):
                        act.wait_ge(s_hfps, 2 * t + half + 1)
                        copy(actT[:, half * 512:(half + 1) * 512], Tb[half][:, :]).then_inc(s_hfT, 1)
                for b in range(PQ_BLOCKS):
                    if k == BLOCK_STEP[IN_BLOCKS + b]:
                        act.wait_ge(s_wused, BLOCKS * t + IN_BLOCKS + b + 1)
                        if b >= 2:
                            act.wait_ge(s_s, PQ_BLOCKS * t + b - 1)
                        copy(pqT[:, (b % 2) * P:(b % 2 + 1) * P], Mb[b % 2][:, 0:P]).then_inc(s_pqT, 1)
                if k == 120:
                    act.wait_ge(s_best, t + 1)
                    act.activation(gate_front[:, :], gate_front[:, :], ACT.Exp).then_inc(s_ge, 1)

            def hand_gates(t):
                act.wait_ge(s_gate, t + 1)
                copy(gate_peer[:, :], gate_front[:, :]).then_inc(s_handg, 1)
                act.wait_ge(s_handg, t + 1)

            def hand_x(t):
                act.wait_ge(s_xm, 2 * t + 2)
                if not first(t):
                    act.wait_ge(s_x2, 1 * t)
                copy(x_peer[:, :], x_front[:, :]).then_inc(s_handx, 1)

            def slot(before, k, gates, eye, rows):
                act.wait_ge(s_dot, before + k + 1)
                act_p.link(act, act.activation(gl[:, k:k + 1], dots[:, k:k + 1], ACT.Gelu))
                act_p.link(act, copy(wk[:, k:k + 1], gl[:, k:k + 1], gates[:, k:k + 1]))
                act.wait_ge(s_slot, before + k + RING - 1)
                copy(diag[:, (k % 2) * P:(k % 2) * P + rows], eye, wk[:, k:k + 1]).then_inc(s_diag, 1)

            def finish(t):
                act.wait_ge(s_x2, t + 1)
                act_y.start(t)
                root(y_buf[:, :], D, SS2, act_y, bufB[:, :]).then_inc(s_ss2, 1)

            def body(t):
                hand_gates(t)
                act_p.start(t)
                for k in range(SLOTS + LAG):
                    if k < SLOTS:
                        slot(SLOTS * t, k, gate_peer, ident[:, :], P)
                    if k == 1:
                        hand_x(t)
                    if k == 3 and not first(t):
                        finish(t - 1)
                    if k >= LAG:
                        front(t + 1, k - LAG)
                act_p.end()

            for k in range(SLOTS):
                front(0, k)
            body(0)
            with act.Fori(1, TILES - 1) as t:
                body(t)
            body(TILES - 1)
            act.wait_ge(s_pack, 16 * 3 * PACK)
            act_p.start(TILES)
            for k in range(PSLOTS):
                slot(SLOTS * TILES, k, gate_pack, fold[:, :], DEC)
                if k == 1:
                    hand_x(S_TILE)
                if k == 3:
                    finish(TILES - 1)
            finish(S_TILE)

        @block.vector
        def _(dve):
            def rstd(c_ss, c_r):
                return dve.reciprocal(col(c_r), col(c_ss))

            def rotate(x, out, n, link):
                c = rope[:, 0:HALF].unsqueeze(1).to_broadcast([P, n, HALF])
                s = rope[:, HALF:ROPE].unsqueeze(1).to_broadcast([P, n, HALF])
                r = [rtmp[:, i * H * HALF:i * H * HALF + n * HALF].rearrange("p (h c) -> p h c", h=n) for i in range(4)]
                x1, x2 = x[:, :, 0:HALF], x[:, :, HALF:ROPE]
                dve.tensor_tensor(r[0], x1, c, ALU.mult)
                dve.tensor_tensor(r[1], x2, s, ALU.mult)
                dve.tensor_tensor(r[2], x1, s, ALU.mult)
                link(dve.tensor_tensor(r[3], x2, c, ALU.mult))
                dve.tensor_tensor(out[:, :, 0:HALF], r[0], r[1], ALU.subtract)
                return dve.tensor_tensor(out[:, :, HALF:ROPE], r[2], r[3], ALU.add)

            def kv_stage(n):
                dve.wait_ge(s_ckps, n + 1)
                dve.tensor_copy(ckT, T1[:, 0:KVR]).then_inc(s_ckT, 1)

            def top16(vals, idx, src, rest, link):
                link(dve.max(vals[:, 0:8], src))
                dve.max_index(idx[:, 0:8], vals[:, 0:8], src)
                link(dve.match_replace(rest, vals[:, 0:8], src, LOWEST))
                link(dve.max(vals[:, 8:16], rest))
                return dve.max_index(idx[:, 8:16], vals[:, 8:16], rest)

            def front(t, k):
                n = S_TILE + 2 if sample(t) else t

                def link(ins):
                    dve_f.link(dve, ins)

                def link_apart(ins):
                    dve_f.link(dve, ins, wait_apart)

                if k == 1:
                    dve.wait_ge(s_ssx, t + 1)
                    rstd(SSX, RX).then_inc(s_rx, 1)
                    if first(t):
                        dve.memset(uT_v[:, :, 0:CK - 1], 0.0).then_inc(s_carry, 1)
                    elif sample(t):
                        dve.tensor_copy(convp[:, :].rearrange("p (j n) -> p j n", j=CC), uT_v[:, :, P:P + CK - 1])
                        dve.tensor_copy(uT_v[:, :, 0:CK - 1], state_v).then_inc(s_carry, 1)
                    else:
                        dve.tensor_copy(uT_v[:, :, 0:CK - 1], uT_v[:, :, P:P + CK - 1]).then_inc(s_carry, 1)
                    if sample(t):
                        dve.tensor_copy(mask[:, 0:PAST + DEC],
                                        zeros[:, 0:1].to_broadcast([P, PAST + DEC]))
                        dve.memset(mask[:, PAST + DEC:KEYS], NEG).then_inc(s_mask, 1)
                    else:
                        if first(t):
                            dve.wait_ge(s_init, 11)
                            dve.tensor_copy(mask[:, 0:P], mask_tile[:, :]).then_inc(s_mask, 1)
                        else:
                            dve.tensor_copy(mask[:, bass.ds((t - 1) * P, P)], zeros[:, :])
                            dve.tensor_copy(mask[:, bass.ds(t * P, P)], mask_tile[:, :]).then_inc(s_mask, 1)
                if k == 3:
                    if first(t):
                        dve.wait_ge(s_const, 16 * 4)
                    for half in range(2):
                        dve.wait_ge(s_hps, 2 * t + half + 1)
                        dve.tensor_tensor(actT_v[:, 4 * half:4 * half + 4, :], v3(Tb[half][:, :], 4),
                                          gain(C_GATTN + 4 * half, 4), ALU.mult).then_inc(s_hT, 1)
                if k == BLOCK_STEP[2] + 1:
                    dve.wait_ge(s_ssz, 2 * t + 1)
                    rstd(SSQ, RQ).then_inc(s_rz, 1)
                if sample(t):
                    for b, part in PAST_STEPS.get(k, ()):
                        if part == 0:
                            kv_stage(TILES + b)
                if k == 10:
                    dve.wait_ge(s_cqps, t + 1)
                    dve.tensor_tensor(v3(cqT, QC), v3(T0[:, 0:QR], QC), gain(C_GQ, QC), ALU.mult).then_inc(s_cqT, 1)
                if k == BLOCK_STEP[5] + 1:
                    dve.wait_ge(s_ssz, 2 * t + 2)
                    link(rstd(SSK, RK))
                    dve.wait_ge(s_rope, 16 * (t + 1))
                    if not first(t):
                        dve.wait_ge(s_kvst, 32 * t)
                    dve.scalar_tensor_tensor(out=ckn[:, 0:KVR], in0=M1[:, 0:KVR], scalar=col(RK), in1=g_kv[:, :],
                                             op0=ALU.mult, op1=ALU.mult)
                    rotate(M1[:, KVR:KVR + ROPE].unsqueeze(1), ckn[:, KVR:KVR + ROPE].unsqueeze(1), 1,
                           link).then_inc(s_ckn, 1)
                if k == 14:
                    kv_stage(n)
                if k == 16:
                    dve.wait_ge(s_qn, 2 * t + 2)
                    pe_part = qn.rearrange("p (h c) -> p h c", h=H)[:, :, NOPE:QK]
                    rotate(pe_part, pe_part, H, link).then_inc(s_qr, 1)
                    dve.wait_ge(s_qr, t + 1)
                    dve.tensor_copy(rtmp[:, 0:1], rope[:, 0:1]).then_inc(s_ropeb, 1)
                if k == 21:
                    for half in range(2):
                        dve.wait_ge(s_qTps, 2 * t + half + 1)
                        dve.tensor_copy(qT[0:QK, half * 512:(half + 1) * 512], Mb[half][0:QK, :]).then_inc(s_qT, 1)
                for j in range(CC):
                    if k == BLOCK_STEP[NAT_BLOCKS + 3 * j + 2] + 1:
                        dve.wait_ge(s_c, CC * t + j + 1)
                        u, o = uT_v[:, j, :], conv_v[:, j, :]
                        w = [cols[:, C_WCONV + CC * i + j:C_WCONV + CC * i + j + 1] for i in range(CK)]
                        link(dve.tensor_tensor(u[:, CK - 1:CK - 1 + P], Sb[j % 2][:, 0:P],
                                               csb[:, (j % 2) * P:(j % 2 + 1) * P], ALU.mult))
                        link(dve.tensor_scalar(o, u[:, 0:P], w[0], None, ALU.mult))
                        for i in (1, 2):
                            link(dve.scalar_tensor_tensor(out=o, in0=u[:, i:i + P], scalar=w[i], in1=o,
                                                          op0=ALU.mult, op1=ALU.add))
                        dve.tensor_tensor(o, o, Sb[j % 2][:, 2 * P:3 * P], ALU.mult).then_inc(s_conv, 1)
                if k == 28:
                    dve.wait_ge(s_conv, CC * t + CC)
                    dve.tensor_tensor(actT_v[:, 4:8, :], conv_v, gain(C_GCONV, CC), ALU.mult).then_inc(s_mixc, 1)
                if k == 31:
                    dve.wait_ge(s_ssc, t + 1)
                    rstd(SSC, RC).then_inc(s_rc, 1)
                for h in range(H):
                    k0 = ATT_STEP + 4 * h
                    if k == k0:
                        dve.wait_ge(s_sc, H * t + h + 1)
                        if h == 0:
                            wait_apart(dve, s_mask, t + 1)
                        else:
                            wait_apart(dve, s_pTps, 2 * H * t + 2 * h)
                        nk = key_blocks(t) * P
                        dve.tensor_tensor_reduce(bufA[:, 0:nk], Sps[:, 0:nk], mask[:, 0:nk], 1.0, LOWEST, ALU.add, ALU.max,
                                                 mx[:, h:h + 1]).then_inc(s_sm, 1)
                        dve.wait_ge(s_sm, H * t + h + 1)
                        dve.tensor_scalar(nm[:, h:h + 1], mx[:, h:h + 1], -SCALE, None, ALU.mult).then_inc(s_nm, 1)
                    if k == k0 + 3:
                        dve.wait_ge(s_pTps, 2 * H * t + 2 * h + 1)
                        if h > 0:
                            dve.wait_ge(s_pv, H * t + h)
                        n_low = min(512, key_blocks(t) * P)
                        dve.tensor_copy(bufB[:, 0:n_low], T0[:, 0:n_low]).then_inc(s_pTa, 1)
                if k == 62:
                    dve.wait_ge(s_pv, H * t + H)
                    link(dve.reciprocal(ri[:, :], rs[:, :]))
                    dve.tensor_tensor(attn[:, :].rearrange("p (h c) -> p h c", h=H),
                                      M1[:, :].rearrange("p (h c) -> p h c", h=H),
                                      ri[:, :].unsqueeze(2).to_broadcast([P, H, VD]), ALU.mult).then_inc(s_at, 1)
                if k == 65:
                    dve.wait_ge(s_ssa, t + 1)
                    link(rstd(SSA, RA))
                    dve.wait_ge(s_aps, t + 1)
                    dve.tensor_tensor(actT_v[:, 0:4, :], v3(T0[:, :], 4), gain(C_GMLA, 4), ALU.mult).then_inc(s_mixa, 1)
                if k in (68, 70):
                    half = (k - 68) // 2
                    x = x_front[:, half * 512:(half + 1) * 512]
                    for i, c in ((0, RA), (1, RC)):
                        dve.wait_ge(s_wo, 4 * t + 2 * half + i + 1)
                        ins = dve.scalar_tensor_tensor(out=x, in0=(S0, S1, T1, M0)[2 * half + i][:, :], scalar=col(c),
                                                       in1=x, op0=ALU.mult, op1=ALU.add)
                        if i == 0:
                            link(ins)
                        else:
                            ins.then_inc(s_xm, 1)
                if k == 72:
                    dve.wait_ge(s_ssm, t + 1)
                    if first(t):
                        dve.wait_ge(s_const2, 16 * 4)
                    link(rstd(SSM, RM))
                    dve.scalar_tensor_tensor(out=hf_front[:, :], in0=x_front[:, :], scalar=col(RM), in1=g_ffn[:, :],
                                             op0=ALU.mult, op1=ALU.mult).then_inc(s_hf, 1)
                for b in range(PQ_BLOCKS):
                    if k == BLOCK_STEP[IN_BLOCKS + b] + 3:
                        wait_apart(dve, s_s, PQ_BLOCKS * t + b + 1)
                        top16(tv[:, b * TOPK:(b + 1) * TOPK], ti[:, b * TOPK:(b + 1) * TOPK],
                              Sb[b % 2][:, 0:P], s2, link_apart).then_inc(s_l1, 1)
                for h in range(PH):
                    if k == BLOCK_STEP[IN_BLOCKS + 2 * h + 1] + 4:
                        dve.wait_ge(s_l1, PQ_BLOCKS * t + 2 * h + 2)
                        va, vb = (tv[:, (2 * h + i) * TOPK:(2 * h + i + 1) * TOPK] for i in range(2))
                        dve.tensor_tensor(cand.rearrange("p (a b) -> p a b", a=TOPK),
                                          va.unsqueeze(2).to_broadcast([P, TOPK, TOPK]),
                                          vb.unsqueeze(1).to_broadcast([P, TOPK, TOPK]), ALU.add)
                        link_apart(dve.tensor_copy(tif[:, :], ti[:, 2 * h * TOPK:(2 * h + 2) * TOPK]))
                        link(top16(best[:, h * TOPK:(h + 1) * TOPK], pos, cand, cand2, link_apart))
                        dve.tensor_scalar(pab[:, 0:TOPK], pos[:, :], 4, None, ALU.logical_shift_right)
                        link(dve.tensor_scalar(pab[:, TOPK:2 * TOPK], pos[:, :], TOPK - 1, None, ALU.bitwise_and))
                        link(dve.tensor_copy(pabf[:, :], pab[:, :]))
                        for i in range(2):
                            link(dve.tensor_tensor(hot, pabf[:, i * TOPK:(i + 1) * TOPK].unsqueeze(2).to_broadcast([P, TOPK, TOPK]),
                                                   iota16[:, :].unsqueeze(1).to_broadcast([P, TOPK, TOPK]), ALU.is_equal))
                            link(dve.tensor_tensor(hot, hot, tif[:, i * TOPK:(i + 1) * TOPK].unsqueeze(1).to_broadcast([P, TOPK, TOPK]),
                                                   ALU.mult))
                            link(dve.tensor_reduce(eab[:, i * TOPK:(i + 1) * TOPK], hot, AX.X, ALU.add))
                        link(dve.scalar_tensor_tensor(out=pabf[:, 0:TOPK], in0=eab[:, 0:TOPK], scalar=float(NKEYS),
                                                      in1=eab[:, TOPK:2 * TOPK], op0=ALU.mult, op1=ALU.add))
                        if h == 0 and not first(t):
                            dve.wait_ge(s_handi, 2 * t)
                        dve.tensor_copy(idx_front[:, h * TOPK:(h + 1) * TOPK], pabf[:, 0:TOPK]).then_inc(s_idx, 1)
                if k == 120:
                    b3 = best[:, :].rearrange("p (h c) -> p h c", h=PH)
                    g3 = gate_front[:, :].rearrange("p (h c) -> p h c", h=PH)
                    if not first(t):
                        dve.wait_ge(s_handg, 1 * t)
                    dve.tensor_tensor(g3, b3, b3[:, :, 0:1].to_broadcast([P, PH, TOPK]), ALU.subtract).then_inc(s_best, 1)
                if k == 121:
                    g3 = gate_front[:, :].rearrange("p (h c) -> p h c", h=PH)
                    dve.wait_ge(s_ge, t + 1)
                    link(dve.tensor_reduce(gsum[:, 0:PH], g3, AX.X, ALU.add))
                    link(dve.reciprocal(gsum[:, PH:2 * PH], gsum[:, 0:PH]))
                    dve.tensor_tensor(g3, g3, gsum[:, PH:2 * PH].unsqueeze(2).to_broadcast([P, PH, TOPK]),
                                      ALU.mult).then_inc(s_gate, 1)

            def whole_front(t, k):
                if k == 0:
                    dve_f.start(t)
                front(t, k)
                if k == SLOTS - 1:
                    dve_f.end()

            def hand(t):
                dve.wait_ge(s_hf, t + 1)
                if not first(t):
                    dve.wait_ge(s_dot, SLOTS * t)
                dve.tensor_copy(hf_peer[:, :], hf_front[:, :]).then_inc(s_handh, 1)
                dve.wait_ge(s_handh, t + 1)

            def slot(t, k, hf):
                dve.wait_ge(s_g[k % RING], 16 * ((SLOTS // RING) * t + k // RING + 1))
                u = ring[k % RING][:, 0:D]
                dve.tensor_tensor_reduce(u, u, hf[:, :], 1.0, 0.0, ALU.mult, ALU.add,
                                         dots[:, k:k + 1]).then_inc(s_dot, 1)

            def add_experts(t):
                rows = slice(0, DEC if sample(t) else P)
                dve.wait_ge(s_slot, RING + SLOTS * TILES + PSLOTS if sample(t) else SLOTS * t + SLOTS + RING)
                dve.wait_ge(s_handx, t + 1)
                if not first(t):
                    dve.wait_ge(s_yst, 16 * t)
                dve.tensor_tensor(y_buf[rows, :], x_peer[rows, :], acc[rows, :], ALU.add).then_inc(s_x2, 1)

            def finish(t):
                rows = slice(0, DEC if sample(t) else P)
                dve_y.start(t)
                dve.wait_ge(s_ss2, t + 1)
                dve_y.link(dve, rstd(SS2, R2))
                dve_y.link(dve, dve.scalar_tensor_tensor(out=y_buf[rows, :], in0=y_buf[rows, :],
                                                         scalar=st[rows, R2:R2 + 1], in1=g_fin[rows, :],
                                                         op0=ALU.mult, op1=ALU.mult))
                dve.sem_inc(s_y, 1)
                dve_y.end()

            def body(t):
                hand(t)
                for k in range(SLOTS + LAG):
                    if k < SLOTS:
                        slot(t, k, hf_peer)
                    if k == 0 and not first(t):
                        add_experts(t - 1)
                    if k == 4 and not first(t):
                        finish(t - 1)
                    if k >= LAG:
                        whole_front(t + 1, k - LAG)

            for k in range(SLOTS):
                whole_front(0, k)
            for q in range(PACK):
                group = slice(q * DEC, (q + 1) * DEC)
                dve.tensor_copy(fold[group, :], ident[group, group]).then_inc(s_fold, 1)
            body(0)
            with dve.Fori(1, TILES - 1) as t:
                body(t)
            body(TILES - 1)
            dve.wait_ge(s_pack, 16 * 3 * PACK)
            for k in range(PSLOTS):
                slot(TILES, k, hf_pack)
                if k == 0:
                    add_experts(TILES - 1)
                if k == 4:
                    finish(TILES - 1)
            add_experts(S_TILE)
            finish(S_TILE)



def blocks(w):
    k, n = w.shape
    return w.reshape(k // P, P, n // P, P).transpose(2, 1, 0, 3).reshape(n // P, P, -1)


def rows(w):
    k, n = w.shape
    return w.reshape(k // P, P, n).transpose(1, 0, 2).reshape(P, -1)


def rope_table():
    at = np.concatenate([np.arange(SEQ), PAST + np.arange(P)]).astype(np.float32)
    freqs = np.float32(10000.0) ** (-np.arange(HALF, dtype=np.float32) / HALF)
    ang = at[:, None] * freqs[None, :].astype(np.float32)
    return np.concatenate([np.cos(ang), np.sin(ang)], axis=1).astype(np.float32)


def kernel(**inputs):
    import concourse.bacc as bacc
    from concourse.bass_utils import run_bass_kernel_spmd

    v = {n: np.asarray(x) for n, x in inputs.items()}
    w_in = v["w_in"][0]
    u0, b0, c0 = NATW, NATW + CW, NATW + 2 * CW
    order = [w_in[:, i * P:(i + 1) * P] for i in range(NAT_BLOCKS - 1)]
    for j in range(CC):
        order += [w_in[:, o + j * P:o + (j + 1) * P] for o in (u0, c0, b0)]
    col = lambda g: g.reshape(-1, P).T
    arrays = {
        "x_p": v["x_prompt"][0],
        "x_s": v["x_sample"][0],
        "c_kv": v["cache_kv_latent"][0, 0],
        "c_pe": v["cache_k_rope"][0, 0],
        "rope": rope_table(),
        "w_str": np.concatenate([blocks(np.concatenate(order, axis=1)), blocks(v["w_peer_q"][0])]),
        "w_nar": rows(w_in[:, NATW - ROPE:NATW]),
        "w_uq": rows(v["w_uq"][0]),
        "w_ukv": rows(v["w_ukv"][0]),
        "w_out": rows(v["w_out"][0]),
        "keysT": v["peer_keys"][0].transpose(3, 0, 1, 2).reshape(P, -1),
        "g_ffn": v["g_ffn_norm"][0],
        "g_fin": v["g_final"],
        "g_kv": v["g_kv"][0],
        "cols": np.concatenate([col(v["g_attn_norm"][0]), col(v["g_q"][0]), col(v["g_mla_out"][0]),
                                col(v["g_conv_out"][0]), *[col(w) for w in v["w_conv"][0]],
                                v["state_conv"][0, 0].reshape(CK - 1, CC, P).transpose(2, 1, 0).reshape(P, -1)],
                               axis=1),
        "uv": np.concatenate([v["peer_u"][0], v["peer_v"][0]], axis=1),
    }
    outs = {
        "o_y_p": (SEQ, D), "o_y_s": (DEC, D), "o_kv_p": (SEQ, KVR), "o_pe_p": (SEQ, ROPE),
        "o_kv_s": (DEC, KVR), "o_pe_s": (DEC, ROPE), "o_cv_p": (P, CC * (CK - 1)), "o_cv_s": (P, CC * (CK - 1)),
    }
    nc = bacc.Bacc("TRN2", target_bir_lowering=False, num_devices=1,
                   dynamic_dma_scratch_size=8192)
    arrays = {n: np.ascontiguousarray(x) for n, x in arrays.items()}
    a = {n: nc.dram_tensor(f"in_{n}", x.shape, F32, kind="ExternalInput").ap() for n, x in arrays.items()}
    a |= {n: nc.dram_tensor(n, s, F32, kind="ExternalOutput").ap() for n, s in outs.items()}
    build(nc, a)
    r = run_bass_kernel_spmd(nc, [{f"in_{n}": x for n, x in arrays.items()}], core_ids=[0]).results[0]
    conv = lambda x: x.reshape(P, CC, CK - 1).transpose(2, 1, 0).reshape(1, 1, CK - 1, CW)
    return (r["o_y_p"].reshape(1, SEQ, D), r["o_y_s"].reshape(1, DEC, D), r["o_kv_p"].reshape(1, 1, SEQ, KVR),
            r["o_pe_p"].reshape(1, 1, SEQ, ROPE), conv(r["o_cv_p"]), r["o_kv_s"].reshape(1, 1, DEC, KVR),
            r["o_pe_s"].reshape(1, 1, DEC, ROPE), conv(r["o_cv_s"]))
```

```python
from contextlib import ExitStack

import numpy as np
import concourse.bass as bass
from concourse import mybir

F32 = mybir.dt.float32
BF16 = mybir.dt.bfloat16
U32 = mybir.dt.uint32
ALU = mybir.AluOpType
ACT = mybir.ActivationFunctionType
AX = mybir.AxisListType

P = 128
D = 1024
KC = D // P
SEQ, DEC, PAST = 1024, 32, 256
TILES = SEQ // P
S_TILE = TILES
CHUNK = 64
EPS = 1e-6
NEG = -1e30
LOWEST = -3.0e38
H, NOPE, ROPE, VD = 8, 64, 32, 64
QK = NOPE + ROPE
HALF = ROPE // 2
SCALE = float(QK) ** -0.5
QR, KVR, CW, CK = 384, 256, 512, 3
QC, CC = QR // P, CW // P
NATW = QR + KVR + ROPE
NKEYS, TOPK, PH = 128, 16, 8
SLOTS = PH * TOPK
KEYS = SEQ
KB = KEYS // P

NAT_BLOCKS = 6
IN_BLOCKS = NAT_BLOCKS + 3 * CC
PQ_BLOCKS = 2 * PH
BLOCKS = IN_BLOCKS + PQ_BLOCKS
NARROW = NAT_BLOCKS - 1
KEPT = (2, 3, 4)
STREAMED = [b for b in range(BLOCKS) if b != NARROW and b not in KEPT]
WBUF = 2
assert len(STREAMED) % WBUF == 0
RING = 4
LEAD = TOPK
PACK = P // DEC
PSLOTS = SLOTS // PACK

STEPS = 128
WOUT_STEPS = (67, 69, 71, 73)
PQ_STEP = 80
BLOCK_STEP = [4 + 4 * b // 3 for b in range(IN_BLOCKS)] + [PQ_STEP + 5 * b // 2 for b in range(PQ_BLOCKS)]
ATT_STEP = 29
SMALL_INITS, INITS = 9, 11
FIRST_ATT_STEP = 24
LAG = 2
FS = 94
OWN = STEPS - FS
FS_FIRST = 90
SAMPLE_SPAN = 85
PAST_STEPS = {6: ((0, 0),), 8: ((0, 1), (0, 2)), 9: ((1, 0),), 11: ((1, 1),), 13: ((1, 2),)}
ACT_FRONT = 5
DVE_FRONT = 192

C_GATTN, C_GQ, C_GMLA, C_GCONV, C_WCONV, C_STATE = 0, 8, 11, 15, 19, 31
NCOLS = 39


def first(t):
    return isinstance(t, int) and t == 0


def front_steps(t, k):
    if k < OWN and first(t):
        lo, hi = (FS_FIRST + (k + i) * (STEPS - FS_FIRST) // OWN for i in range(2))
        return [(t, j) for j in range(lo, hi)]
    if k < OWN:
        return [(t, FS + k)]
    nxt = t + 1
    if sample(nxt):
        lo, hi = ((k - OWN + i) * STEPS // SAMPLE_SPAN for i in range(2))
        return [(nxt, j) for j in range(lo, min(hi, STEPS))]
    return [(nxt, k - OWN)]


def key_blocks(t):
    return PAST // P + 1 if sample(t) else KB


def sample(t):
    return isinstance(t, int) and t == S_TILE


def tokens(t):
    return DEC if sample(t) else P


class Count:

    def __init__(self, sem, per):
        self.sem, self.per = sem, per
        self.marks = {}

    def start(self, t, step=0):
        self.n = self.marks.setdefault(step, self.n if step else 0)
        self.t = t

    def link(self, eng, ins, wait=None):
        self.n += 1
        ins.then_inc(self.sem, 1)
        (wait or type(eng).wait_ge)(eng, self.sem, self.per * self.t + self.n)

    def end(self):
        assert self.n == self.per, (self.n, self.per)


def build(nc, a):
    with ExitStack() as ctx:
        def sb(name, cols, dt=F32):
            return ctx.enter_context(nc.sbuf_tensor(name, [P, cols], dt))

        def psum(name):
            return ctx.enter_context(nc.psum_tensor(name, [P, 512], F32))

        def sem(name):
            return ctx.enter_context(nc.semaphore(name))

        w_out = sb("w_out_sb", KC * D)
        w_uq = sb("w_uq_sb", QC * H * QK)
        w_ukv = sb("w_ukv_sb", 2 * H * (NOPE + VD))
        keysT = sb("keysT_sb", PQ_BLOCKS * NKEYS)
        g_ffn = sb("g_ffn_sb", D)
        g_fin = sb("g_fin_sb", D)
        g_kv = sb("g_kv_sb", KVR)
        cols = sb("cols_sb", NCOLS)
        kT = sb("kT", H * KEYS)
        vv = sb("vv", KB * H * VD)
        w_narrow = sb("w_narrow_sb", KC * ROPE)
        w_kept = [sb(f"w_kept{b}", KC * P) for b in KEPT]
        wst = [sb(f"wst{i}", KC * P) for i in range(WBUF)]
        ring_u = [sb(f"ring_u{i}", D) for i in range(RING)]
        ring_v = [sb(f"ring_v{i}", D) for i in range(RING)]
        x_front = sb("x_front", D)
        x_peer = sb("x_peer", D)
        hf_front = sb("hf_front", D)
        hf_peer = sb("hf_peer", D)
        idx_s = sb("idx_s", SLOTS, U32)
        idx_peer = sb("idx_peer", SLOTS, U32)
        idx_lead = sb("idx_lead", LEAD, U32)
        idx_pack = sb("idx_pack", PSLOTS, U32)
        gate_pack = sb("gate_pack", PSLOTS)
        gate_s = sb("gate_s", SLOTS)
        gate_peer = sb("gate_peer", SLOTS)
        rope = sb("rope", ROPE)
        actT = sb("actT", KC * P)
        ckn = sb("ckn", KVR + ROPE)
        qT = sb("qT", H * P)
        cqT = qT[:, 0:QR]
        ckT = qT[:, QR:QR + KVR]
        y_buf = qT
        uT = sb("uT", CC * (P + CK - 1))
        convT = sb("convT", CW)
        attn = convT
        convp = sb("convp", CC * (CK - 1))
        csb = sb("csb", 2 * P)
        mask = sb("mask", KEYS, BF16)
        mask_tile = sb("mask_tile", P, BF16)
        zeros = sb("zeros", P, BF16)
        ident = sb("ident", P)
        fold = sb("fold", DEC)
        ones = sb("ones", 1)
        bufA = sb("bufA", D)
        bufB = sb("bufB", D)
        diag = sb("diag", 2 * P)
        rtmp = bufA[:, D - 4 * H * HALF:D]
        tv = sb("tv", PQ_BLOCKS * TOPK)
        ti = sb("ti", PQ_BLOCKS * TOPK, U32)
        tif = sb("tif", 2 * TOPK)
        best = sb("best", SLOTS)
        pos = sb("pos", TOPK, U32)
        pab = sb("pab", 2 * TOPK, U32)
        pabf = sb("pabf", 2 * TOPK)
        eab = sb("eab", 2 * TOPK)
        iota16 = sb("iota16", TOPK)
        gsum = sb("gsum", 2 * PH)
        dots = sb("dots", SLOTS)
        st = sb("st", 24)
        mx = sb("mx", H)
        nm = sb("nm", H)
        rs = sb("rs", H)
        ri = sb("ri", H)

        acc = ctx.enter_context(nc.psum_tensor("acc", [P, 2 * 512], F32))
        Sps = ctx.enter_context(nc.psum_tensor("Sps", [P, 2 * 512], F32))
        S0, S1 = Sps[:, 0:512], Sps[:, 512:1024]
        T0, T1, M0, M1 = [psum(n) for n in ("T0", "T1", "M0", "M1")]

        s_passed = {e: sem(f"s_passed_{e}") for e in ("pool", "dve")}

        def wait_apart(eng, s, value):
            eng.wait_ge(s, value)
            eng.sem_inc(s_passed["pool" if eng is nc.gpsimd else "dve"], 1)

        s_const = sem("s_const")
        s_narrow = sem("s_narrow_loaded")
        s_kept = sem("s_kept_loaded")
        s_up = sem("s_up_loaded")
        s_out = sem("s_w_out_loaded")
        s_late = sem("s_late_loaded")
        s_x = sem("s_x_loaded")
        s_rope = sem("s_rope_loaded")
        s_w = [sem(f"s_w_loaded{i}") for i in range(WBUF)]
        s_wused = sem("s_w_used")
        s_past = sem("s_past_loaded")
        s_kvst = sem("s_kv_stored")
        s_cpst = sem("s_conv_stored")
        s_yst = sem("s_y_stored")
        s_gu = [sem(f"s_u_gathered{i}") for i in range(RING)]
        s_gv = [sem(f"s_v_gathered{i}") for i in range(RING)]
        s_init = sem("s_init")
        s_fold = sem("s_fold")
        s_ropeb = sem("s_rope_used")
        s_ssx = sem("s_ssx")
        s_rx = sem("s_rx")
        s_h = sem("s_h")
        s_hps = sem("s_h_turned")
        s_hT = sem("s_hT")
        s_ssz = sem("s_ssz")
        s_rz = sem("s_rz")
        s_cqn = sem("s_cqn")
        s_ckn = sem("s_ckn")
        s_cqps = sem("s_cq_turned")
        s_cqT = sem("s_cqT")
        s_ckps = sem("s_ck_turned")
        s_ckT = sem("s_ckT")
        s_kpe = sem("s_kpe")
        s_kvps = sem("s_kv_ps")
        s_kv = sem("s_kv_kept")
        s_qps = sem("s_q_ps")
        s_qn = sem("s_qn")
        s_qr = sem("s_q_rotated")
        s_qTps = sem("s_q_turned")
        s_qT = sem("s_qT")
        s_c = sem("s_c")
        s_conv = sem("s_conv")
        s_carry = sem("s_carry")
        s_csq = sem("s_csq")
        s_mixc = sem("s_mixc")
        s_css = sem("s_css")
        s_ssc = sem("s_ssc")
        s_rc = sem("s_rc")
        s_mask = sem("s_mask")
        s_sc = sem("s_scores")
        s_sm = sem("s_masked")
        s_nm = sem("s_negmax")
        s_p = sem("s_probs")
        s_pTps = sem("s_p_turned")
        s_pTa = sem("s_pT_low")
        s_pTb = sem("s_pT_high")
        s_pv = sem("s_pv")
        s_at = sem("s_attn")
        s_ssa = sem("s_ssa")
        s_aps = sem("s_attn_turned")
        s_mixa = sem("s_mixa")
        s_wo = sem("s_wo")
        s_xm = sem("s_xmid")
        s_ssm = sem("s_ssm")
        s_hf = sem("s_hf")
        s_hfps = sem("s_hf_turned")
        s_hfT = sem("s_hfT")
        s_pqT = sem("s_pqT")
        s_s = sem("s_keyscores")
        s_l1 = sem("s_level1")
        s_idx = sem("s_idx")
        s_best = sem("s_best")
        s_ge = sem("s_gate_exp")
        s_gate = sem("s_gate")
        s_handx = sem("s_hand_x")
        s_handh = sem("s_hand_hf")
        s_pack = sem("s_packed")
        s_dot = sem("s_dot")
        s_diag = sem("s_diag")
        s_slot = sem("s_slot_done")
        s_x2 = sem("s_x2")
        s_ss2 = sem("s_ss2")
        s_y = sem("s_y")
        dve_f = Count(sem("s_dve_front"), DVE_FRONT)
        act_f = Count(sem("s_act_front"), ACT_FRONT)
        act_y = Count(sem("s_act_final"), 1)
        act_p = Count(sem("s_act_peer"), 2 * SLOTS)
        dve_y = Count(sem("s_dve_final"), 2)

        w_out_v = w_out[:, :].rearrange("p (k n) -> p k n", k=KC)
        w_uq_v = w_uq[:, :].rearrange("p (k n) -> p k n", k=QC)
        w_ukv_v = w_ukv[:, :].rearrange("p (k h c) -> p k h c", k=2, h=H)
        keysT_v = keysT[:, :].rearrange("p (b n) -> p b n", b=PQ_BLOCKS)

        def block_view(b):
            w = w_narrow if b == NARROW else w_kept[KEPT.index(b)] if b in KEPT else wst[STREAMED.index(b) % WBUF]
            return w[:, :].rearrange("p (k n) -> p k n", k=KC)

        kT_v = kT[:, :].rearrange("p (h k) -> p h k", h=H)
        actT_v = actT[:, :].rearrange("p (k n) -> p k n", k=KC)
        uT_v = uT[:, :].rearrange("p (j n) -> p j n", j=CC)
        conv_v = convT[:, :].rearrange("p (j n) -> p j n", j=CC)
        state_v = cols[:, C_STATE:C_STATE + 8].rearrange("p (j n) -> p j n", j=CC)
        past = bufA[:, 448:1024].rearrange("p (b n) -> p b n", b=2)

        def csq_of(t):
            return (hf_front if first(t) else bufB)[:, 0:CW].rearrange("p (j n) -> p j n", j=CC)

        hnat = bufA
        hf_pack = bufA
        cqn = bufA[:, 0:QR]
        qn = bufB[:, 0:H * QK]
        pqT = bufB[:, 0:2 * P]
        s2 = bufA[:, 0:128]
        cand = bufA[:, 128:384]
        cand2 = bufA[:, 384:640]
        hot = bufA[:, 640:896].rearrange("p (k c) -> p k c", c=TOPK)
        Sb = [S0, S1]
        Tb = [T0, T1]
        Mb = [M0, M1]
        SSX, RX, SSQ, RQ, SSK, RK, RC, SSA, RA, SSM, RM, SS2, R2, SSC, EPSC = range(15)

        def col(c):
            return st[:, c:c + 1]

        def gain(c, n):
            return cols[:, c:c + n].unsqueeze(2).to_broadcast([P, n, P])

        def v3(ap, n):
            return ap.rearrange("p (k n) -> p k n", k=n)

        block = ctx.enter_context(nc.Block())

        @block.sync
        def _(sp):
            def load_block(t, b):
                i = STREAMED.index(b)
                if i >= WBUF:
                    sp.wait_ge(s_wused, BLOCKS * t + STREAMED[i - WBUF] + 1)
                elif not first(t):
                    sp.wait_ge(s_wused, BLOCKS * t - BLOCKS + STREAMED[i - WBUF] + 1)
                sp.dma_start(wst[i % WBUF][:, :], a["w_blocks"][b - (b > NARROW)]).then_inc(s_w[i % WBUF], 16)

            def front(t, k):
                if k == 0:
                    if not first(t):
                        sp.wait_ge(s_handx, t)
                    if sample(t):
                        sp.dma_start(x_front[0:DEC, :], a["x_s"]).then_inc(s_x, 16)
                    else:
                        sp.dma_start(x_front[:, :], a["x_p"][bass.ds(t * P, P), :]).then_inc(s_x, 16)
                    if not first(t):
                        sp.wait_ge(s_ropeb, 1 * t)
                    sp.dma_start(rope[:, :], a["rope"][bass.ds(t * P, P), :]).then_inc(s_rope, 16)
                for b in STREAMED:
                    if max(0, BLOCK_STEP[b] - 4) == k:
                        load_block(t, b)
                if sample(t) and k == 4:
                    sp.wait_ge(s_hps, 2 * t + 2)
                    sp.dma_start(past[:, :, 0:KVR], a["c_kv"].rearrange("(b p) n -> p b n", p=P)).then_inc(s_past, 16)
                    sp.dma_start(past[:, :, KVR:KVR + ROPE],
                                 a["c_pe"].rearrange("(b p) n -> p b n", p=P)).then_inc(s_past, 16)
                if k == 22:
                    sp.wait_ge(s_ckn, t + 1)
                    if sample(t):
                        sp.dma_start(a["o_kv_s"], ckn[0:DEC, 0:KVR]).then_inc(s_kvst, 16)
                        sp.dma_start(a["o_pe_s"], ckn[0:DEC, KVR:KVR + ROPE]).then_inc(s_kvst, 16)
                    else:
                        sp.dma_start(a["o_kv_p"][bass.ds(t * P, P), :], ckn[:, 0:KVR]).then_inc(s_kvst, 16)
                        sp.dma_start(a["o_pe_p"][bass.ds(t * P, P), :], ckn[:, KVR:KVR + ROPE]).then_inc(s_kvst, 16)
                if k == 40 and sample(t):
                    sp.wait_ge(s_carry, S_TILE + 1)
                    sp.dma_start(a["o_cv_p"], convp[:, :]).then_inc(s_cpst, 16)
                    sp.wait_ge(s_conv, CC * (t + 1))
                    sp.dma_start(a["o_cv_s"].rearrange("p (j n) -> p j n", j=CC),
                                 uT_v[:, :, DEC:DEC + CK - 1]).then_inc(s_cpst, 16)

            def store_y(t):
                sp.wait_ge(s_y, t + 1)
                if sample(t):
                    sp.dma_start(a["o_y_s"], y_buf[0:DEC, :]).then_inc(s_yst, 16)
                else:
                    sp.dma_start(a["o_y_p"][bass.ds(t * P, P), :], y_buf[:, :]).then_inc(s_yst, 16)

            sp.dma_start(cols[:, :], a["cols"]).then_inc(s_const, 16)
            front(0, 0)
            sp.dma_start(g_kv[:, :], a["g_kv"].partition_broadcast(P)).then_inc(s_const, 16)
            for w, b in zip(w_kept, KEPT):
                sp.dma_start(w[:, :], a["w_blocks"][b - (b > NARROW)]).then_inc(s_kept, 16)
            pieces = [(s_narrow, w_narrow[:, :], a["w_narrow"])]
            pieces += [(s_up, w_uq[:, c * H * QK:(c + 1) * H * QK], a["w_uq"][:, c * H * QK:(c + 1) * H * QK])
                      for c in range(QC)]
            pieces += [(s_up, w_ukv[:, c * D:(c + 1) * D], a["w_ukv"][:, c * D:(c + 1) * D]) for c in range(2)]
            pieces += [(s_out, w_out[:, c * D:(c + 1) * D], a["w_out"][:, c * D:(c + 1) * D]) 
                       for c in (4, 5, 6, 7, 0, 1, 2, 3)]
            pieces += [(s_late, g_ffn[:, :], a["g_ffn"].partition_broadcast(P))]
            pieces += [(s_late, keysT[:, c * D:(c + 1) * D], a["keysT"][:, c * D:(c + 1) * D]) for c in range(2)]
            pieces += [(s_late, g_fin[:, :], a["g_fin"].partition_broadcast(P))]
            for k in range(1, FS_FIRST):
                front(0, k)
                if pieces and k > 1:
                    landed, dst, src = pieces.pop(0)
                    sp.dma_start(dst, src).then_inc(landed, 16)
            assert not pieces

            def body(t):
                for k in range(SLOTS):
                    for tile, step in front_steps(t, k):
                        front(tile, step)
                    if k == 8 and not first(t):
                        store_y(t - 1)

            body(0)
            with sp.Fori(1, TILES - 1) as t:
                body(t)
            body(TILES - 1)
            sp.wait_ge(s_idx, PH * (S_TILE + 1))
            sp.wait_ge(s_gate, PH * (S_TILE + 1))
            for q in range(PACK):
                group = slice(q * DEC, (q + 1) * DEC)
                part = slice(q * PSLOTS, (q + 1) * PSLOTS)
                sp.dma_start(idx_pack[group, :], idx_s[0:DEC, part]).then_inc(s_pack, 16)
                sp.dma_start(gate_pack[group, :], gate_s[0:DEC, part]).then_inc(s_pack, 16)
                sp.dma_start(hf_pack[group, :], hf_front[0:DEC, :]).then_inc(s_pack, 16)
            store_y(TILES - 1)
            store_y(S_TILE)
            sp.wait_ge(s_yst, 16 * (S_TILE + 1))
            sp.wait_ge(s_kvst, 32 * (S_TILE + 1))
            sp.wait_ge(s_cpst, 32)

        @block.gpsimd
        def _(pool):
            pool.memset(ident[:, :], 0.0).then_inc(s_init, 1)
            pool.memset(mask_tile[:, :], 0.0).then_inc(s_init, 1)
            pool.memset(ones[:, :], 1.0).then_inc(s_init, 1)
            pool.memset(zeros[:, :], 0.0).then_inc(s_init, 1)
            pool.iota(iota16[:, :], pattern=[[1, TOPK]], base=0, channel_multiplier=0,
                      allow_small_or_imprecise_dtypes=True).then_inc(s_init, 1)
            pool.wait_ge(s_init, 5)
            pool.affine_select(out=ident[:, :], in_=ident[:, :], compare_op=ALU.not_equal, fill=1.0, base=0,
                               pattern=[[-1, P]], channel_multiplier=1).then_inc(s_init, 1)
            pool.memset(mask_tile[0:CHUNK, CHUNK:P], NEG).then_inc(s_init, 1)
            pool.sem_inc(s_slot, RING)
            pool.memset(col(EPSC), EPS).then_inc(s_init, 1)
            pool.memset(mask[:, :], NEG).then_inc(s_init, 1)
            pool.memset(kT[:, :], 0.0).then_inc(s_init, 1)
            pool.memset(vv[:, :], 0.0).then_inc(s_init, 1)

            def gather(ring, table, sem, tile, k):
                src = idx_pack if sample(tile) else idx_lead if k < LEAD else idx_peer
                pool.indirect_dma_start(ring[k % RING][:, :], None, table,
                                        bass.IndirectOffsetOnAxis(ap=src[:, k:k + 1], axis=0)
                                        ).then_inc(sem[k % RING], 16)

            def gathers(tile, before, n):
                for k in range(n + 1):
                    if k < n:
                        if k % TOPK == 0 and not sample(tile):
                            wait_apart(pool, s_idx, PH * tile + k // TOPK + 1)
                        if not first(tile) or k >= RING:
                            wait_apart(pool, s_dot, before + k - RING + 1)
                        gather(ring_u, a["peer_u"], s_gu, tile, k)
                    if k >= 1:
                        wait_apart(pool, s_slot, before + k)
                        gather(ring_v, a["peer_v"], s_gv, tile, k - 1)

            gathers(0, 0, SLOTS)
            with pool.Fori(1, TILES - 1) as t:
                gathers(t, SLOTS * t, SLOTS)
            gathers(TILES - 1, SLOTS * (TILES - 1), SLOTS)
            pool.wait_ge(s_pack, 16 * 3 * PACK)
            gathers(S_TILE, SLOTS * TILES, PSLOTS)

        @block.tensor
        def _(pe):
            def turn(dst, src):
                return pe.transpose(dst, src, ident[:, :])

            def w_ready(t, b):
                if b in STREAMED:
                    i = STREAMED.index(b)
                    pe.wait_ge(s_w[i % WBUF], 16 * ((len(STREAMED) // WBUF) * t + i // WBUF + 1))
                elif first(t):
                    if b == NARROW:
                        pe.wait_ge(s_narrow, 16)
                    else:
                        pe.wait_ge(s_kept, 16 * len(KEPT))

            def in_block(t, b):
                w_ready(t, b)
                w = block_view(b)
                if b < NAT_BLOCKS:
                    n = ROPE if b == NAT_BLOCKS - 1 else P
                    bank = Mb[b // QC]
                    at = (b % QC) * P
                    if b % QC == 0 and not first(t):
                        pe.wait_ge(s_pqT, PQ_BLOCKS * t)
                    for c in range(KC):
                        mm = pe.matmul(bank[:, at:at + n], actT_v[:, c, :], w[:, c, 0:n],
                                       start=(c == 0), stop=(c == KC - 1))
                    mm.then_inc(s_wused, 1)
                else:
                    j, part = divmod(b - NAT_BLOCKS, 3)
                    bank = Sb[j % 2]
                    if part == 0:
                        if j >= 2:
                            pe.wait_ge(s_conv, CC * t + j - 1)
                        elif not first(t):
                            pe.wait_ge(s_l1, PQ_BLOCKS * t)
                            if sample(t):
                                pe.wait_ge(s_kv, 3 * (TILES + 1) + 2)
                    n = tokens(t)
                    for c in range(KC):
                        mm = pe.matmul(bank[:, part * P:part * P + n], w[:, c, :], actT_v[:, c, 0:n],
                                       start=(c == 0), stop=(c == KC - 1))
                    mm.then_inc(s_wused, 1)

            def kv_stage(n, src, k):
                if k == 0:
                    if not first(n):
                        pe.wait_ge(s_kv, 3 * n)
                    for i, (lo, hi) in enumerate(((0, P), (P, 2 * P), (KVR + ROPE - QK, KVR + ROPE))):
                        mm = turn(T1[0:hi - lo, i * P:(i + 1) * P], src[:, lo:hi])
                    mm.then_inc(s_ckps, 1)
                if k == 1:
                    pe.wait_ge(s_ckT, n + 1)
                    pe.wait_ge(s_kpe, n + 1)
                    banks = Sb if src is not ckn else Tb
                    for half in range(2):
                        for h in range(4):
                            for c in range(2):
                                mm = pe.matmul(banks[half][0:NOPE, h * P:(h + 1) * P], w_ukv_v[:, c, 4 * half + h, 0:NOPE],
                                               ckT[:, c * P:(c + 1) * P], start=(c == 0), stop=(c == 1))
                        mm.then_inc(s_kvps, 1)
                if k == 2:
                    if src is ckn:
                        pe.wait_ge(s_kv, 3 * n + 1)
                    elif n == TILES + 1:
                        pe.wait_ge(s_cqT, S_TILE + 1)
                    for c in range(2):
                        mm = pe.matmul(T0[:, :].rearrange("p (h c) -> p h c", h=H), ckT[:, c * P:(c + 1) * P],
                                       w_ukv_v[:, c, :, NOPE:NOPE + VD], start=(c == 0), stop=(c == 1))
                    mm.then_inc(s_kvps, 1)

            def out_product(bank, mixer, half):
                for c in range(4):
                    mm = pe.matmul(bank, actT_v[:, 4 * mixer + c, :],
                                   w_out_v[:, 4 * mixer + c, half * 512:(half + 1) * 512],
                                   start=(c == 0), stop=(c == 3))
                mm.then_inc(s_wo, 1)

            def front(t, k):
                n = S_TILE + 2 if sample(t) else t
                if k == 3:
                    pe.wait_ge(s_h, t + 1)
                    if first(t):
                        pe.wait_ge(s_init, SMALL_INITS)
                        pe.wait_ge(s_const, 16 * 2)
                    for c in range(KC):
                        mm = turn(Tb[c // 4][:, (c % 4) * P:(c % 4 + 1) * P], hnat[:, c * P:(c + 1) * P])
                        if c % 4 == 3:
                            mm.then_inc(s_hps, 1)
                if k == BLOCK_STEP[0]:
                    pe.wait_ge(s_hT, 2 * t + 2)
                if sample(t):
                    if k == 6:
                        pe.wait_ge(s_past, 32)
                    for b, part in PAST_STEPS.get(k, ()):
                        kv_stage(TILES + b, past[:, b, :], part)
                if k == 10:
                    pe.wait_ge(s_cqn, t + 1)
                    if sample(t):
                        pe.wait_ge(s_kv, 3 * TILES + 3)
                    for c in range(QC):
                        mm = turn(T0[:, c * P:(c + 1) * P], cqn[:, c * P:(c + 1) * P])
                    mm.then_inc(s_cqps, 1)
                if k == 14:
                    pe.wait_ge(s_ckn, t + 1)
                    kv_stage(n, ckn, 0)
                if k in (13, 15):
                    half = (k - 13) // 2
                    if half == 0:
                        if first(t):
                            pe.wait_ge(s_up, 16 * (QC + 2))
                        pe.wait_ge(s_cqT, t + 1)
                    else:
                        pe.wait_ge(s_ckn, t + 1)
                    for c in range(QC):
                        mm = pe.matmul(Mb[half][:, 0:QR], cqT[:, c * P:(c + 1) * P],
                                       w_uq_v[:, c, half * QR:(half + 1) * QR], start=(c == 0), stop=(c == QC - 1))
                    mm.then_inc(s_qps, 1)
                if k == 19:
                    kv_stage(n, ckn, 1)
                if k == 23:
                    kv_stage(n, ckn, 2)
                if k == (FIRST_ATT_STEP - 2 if first(t) else 26):
                    pe.wait_ge(s_qr, t + 1)
                    for h in range(H):
                        mm = turn(Mb[h // 4][0:QK, (h % 4) * P:(h % 4 + 1) * P], qn[:, h * QK:(h + 1) * QK])
                        if h % 4 == 3:
                            mm.then_inc(s_qTps, 1)
                for b in range(IN_BLOCKS):
                    if BLOCK_STEP[b] == k:
                        in_block(t, b)
                if k == 30:
                    csq = csq_of(t)
                    pe.wait_ge(s_csq, t + 1)
                    pe.wait_ge(s_kv, 3 * n + 3)
                    for j in range(CC):
                        mm = pe.matmul(T1[:, 0:1], csq[:, j, :], ones[:, 0:1], start=(j == 0), stop=(j == CC - 1))
                    mm.then_inc(s_css, 1)
                if first(t):
                    if k == FIRST_ATT_STEP:
                        pe.wait_ge(s_qT, 2)
                        pe.wait_ge(s_kv, 3)
                        for h in range(H):
                            mm = pe.matmul(acc[:, h * P:(h + 1) * P], qT[0:QK, h * P:(h + 1) * P],
                                           kT_v[0:QK, h, 0:P], start=True, stop=True)
                        mm.then_inc(s_sc, H)
                    if k == FIRST_ATT_STEP + 3:
                        pe.wait_ge(s_p, H)
                        for h in range(H):
                            mm = turn(Tb[h // 4][:, (h % 4) * P:(h % 4 + 1) * P], bufA[:, h * P:(h + 1) * P])
                            if h % 4 == 3:
                                mm.then_inc(s_pTps, H)
                    if k == FIRST_ATT_STEP + 5:
                        pe.wait_ge(s_pTa, H)
                        pe.wait_ge(s_pTb, H)
                        for h in range(H):
                            mm = pe.matmul(M1[:, h * VD:(h + 1) * VD], bufB[:, h * P:(h + 1) * P],
                                           vv[:, h * VD:(h + 1) * VD], start=True, stop=True)
                        mm.then_inc(s_pv, H)
                nb = key_blocks(t)
                for h in range(0 if first(t) else H):
                    k0 = ATT_STEP + 4 * h
                    if k == k0:
                        if h == 0:
                            pe.wait_ge(s_qT, 2 * t + 2)
                            pe.wait_ge(s_conv, CC * t + CC)
                        else:
                            pe.wait_ge(s_sm, H * t + h)
                        for lo in range(0, nb * P, 512):
                            n_keys = min(512, nb * P - lo)
                            mm = pe.matmul(Sps[:, lo:lo + n_keys], qT[0:QK, h * P:(h + 1) * P],
                                           kT_v[0:QK, h, lo:lo + n_keys], start=True, stop=True)
                        mm.then_inc(s_sc, 1)
                    if k == k0 + 3:
                        pe.wait_ge(s_p, H * t + h + 1)
                        if h == 0:
                            pe.wait_ge(s_rc, t + 1)
                        else:
                            pe.wait_ge(s_pTa, H * t + h)
                            pe.wait_ge(s_pTb, H * t + h)
                        for c in range(nb):
                            mm = turn(Tb[c // 4][:, (c % 4) * P:(c % 4 + 1) * P], bufA[:, c * P:(c + 1) * P])
                            if c == nb - 1 or c == 3:
                                mm.then_inc(s_pTps, 1 if nb > 4 else 2)
                    if k == k0 + 5:
                        pe.wait_ge(s_pTa, H * t + h + 1)
                        pe.wait_ge(s_pTb, H * t + h + 1)
                        for c in range(nb):
                            mm = pe.matmul(M1[:, h * VD:(h + 1) * VD], bufB[:, c * P:(c + 1) * P],
                                           vv[:, (c * H + h) * VD:(c * H + h + 1) * VD],
                                           start=(c == 0), stop=(c == nb - 1))
                        mm.then_inc(s_pv, 1)
                if k == 65:
                    pe.wait_ge(s_at, t + 1)
                    for c in range(4):
                        mm = turn(T0[:, c * P:(c + 1) * P], attn[:, c * P:(c + 1) * P])
                    mm.then_inc(s_aps, 1)
                if first(t) and k in (29, 33):
                    half = k // 33
                    pe.wait_ge(s_out, 16 * KC)
                    pe.wait_ge(s_mixc, 1)
                    pe.wait_ge(s_sm, H)
                    out_product(acc[:, half * 512:(half + 1) * 512], 1, half)
                if k in WOUT_STEPS and not (first(t) and WOUT_STEPS.index(k) % 2 == 1):
                    i = WOUT_STEPS.index(k)
                    if i == 0:
                        pe.wait_ge(s_mixa, t + 1)
                        pe.wait_ge(s_mixc, t + 1)
                        pe.wait_ge(s_rc, t + 1)
                        pe.wait_ge(s_sm, H * t + H)
                    out_product((S0, S1, T1, M0)[i][:, :], i % 2, i // 2)
                if k == 78:
                    pe.wait_ge(s_hf, t + 1)
                    for c in range(KC):
                        mm = turn(Tb[c // 4][:, (c % 4) * P:(c % 4 + 1) * P], hf_front[:, c * P:(c + 1) * P])
                        if c % 4 == 3:
                            mm.then_inc(s_hfps, 1)
                for b in range(PQ_BLOCKS):
                    if k == BLOCK_STEP[IN_BLOCKS + b]:
                        if b == 0:
                            pe.wait_ge(s_hfT, 2 * t + 2)
                        if b >= 2:
                            pe.wait_ge(s_pqT, PQ_BLOCKS * t + b - 1)
                        w_ready(t, IN_BLOCKS + b)
                        w = block_view(IN_BLOCKS + b)
                        n = tokens(t)
                        for c in range(KC):
                            mm = pe.matmul(Mb[b % 2][:, 0:n], w[:, c, :], actT_v[:, c, 0:n],
                                           start=(c == 0), stop=(c == KC - 1))
                        mm.then_inc(s_wused, 1)
                    if k == BLOCK_STEP[IN_BLOCKS + b] + 3:
                        pe.wait_ge(s_pqT, PQ_BLOCKS * t + b + 1)
                        if b >= 2:
                            pe.wait_ge(s_l1, PQ_BLOCKS * t + b - 1)
                        pe.matmul(Sb[b % 2][:, 0:P], pqT[:, (b % 2) * P:(b % 2 + 1) * P],
                                  keysT_v[:, b, :], start=True, stop=True).then_inc(s_s, 1)

            def slot(t, k, n, rows):
                pe.wait_ge(s_diag, SLOTS * t + k + 1)
                pe.wait_ge(s_gv[k % RING], 16 * ((SLOTS // RING) * t + k // RING + 1))
                for half in range(2):
                    mm = pe.matmul(acc[0:rows, half * 512:(half + 1) * 512], diag[:, (k % 2) * P:(k % 2) * P + rows],
                                   ring_v[k % RING][:, half * 512:(half + 1) * 512],
                                   start=(k == 0), stop=(k == n - 1))
                mm.then_inc(s_slot, 1)

            def body(t):
                for k in range(SLOTS):
                    if k == 0 and not first(t):
                        pe.wait_ge(s_x2, 1 * t)
                    slot(t, k, SLOTS, P)
                    for tile, step in front_steps(t, k):
                        front(tile, step)

            for k in range(FS_FIRST):
                front(0, k)
            body(0)
            with pe.Fori(1, TILES - 1) as t:
                body(t)
            body(TILES - 1)
            pe.wait_ge(s_x2, TILES)
            for k in range(PSLOTS):
                slot(S_TILE, k, PSLOTS, DEC)

        @block.scalar
        def _(act):
            def copy(out, in_, scale=1.0):
                return act.activation(out, in_, ACT.Copy, scale=scale)

            def root(src, n, c, count, junk):
                count.link(act, act.activation(junk, src, ACT.Square, accum_out=col(c)))
                return act.activation(col(c), col(c), ACT.Sqrt, bias=col(EPSC), scale=1.0 / n)

            def kv_stage(n, at, k):
                if k == 0:
                    act.wait_ge(s_ckT, n + 1)
                    copy(kT_v[NOPE:QK, :, bass.ds(at * P, P)],
                         T1[NOPE:QK, 2 * P:3 * P].unsqueeze(1).to_broadcast([ROPE, H, P])).then_inc(s_kpe, 1)
                if k == 1:
                    for half in range(2):
                        act.wait_ge(s_kvps, 3 * n + half + 1)
                        banks = Sb if isinstance(n, int) and TILES <= n < TILES + 2 else Tb
                        copy(kT_v[0:NOPE, 4 * half:4 * half + 4, bass.ds(at * P, P)],
                             v3(banks[half][0:NOPE, :], 4)).then_inc(s_kv, 1)
                if k == 2:
                    act.wait_ge(s_kvps, 3 * n + 3)
                    copy(vv[:, bass.ds(at * 512, 512)], T0[:, :]).then_inc(s_kv, 1)

            def front(t, k):
                n = S_TILE + 2 if sample(t) else t
                at = PAST // P if sample(t) else t
                act_f.start(t, k)
                if k == STEPS - 1:
                    act_f.end()
                if k == 0:
                    if first(t):
                        act.wait_ge(s_init, SMALL_INITS)
                if k == 1:
                    act.wait_ge(s_x, 16 * (t + 1))
                    root(x_front[:, :], D, SSX, act_f, bufB[:, :]).then_inc(s_ssx, 1)
                if k == 2:
                    act.wait_ge(s_rx, t + 1)
                    copy(hnat[:, :], x_front[:, :], col(RX)).then_inc(s_h, 1)
                if sample(t):
                    for b, part in PAST_STEPS.get(k, ()):
                        kv_stage(TILES + b, b, part)
                if k == BLOCK_STEP[2]:
                    act.wait_ge(s_wused, BLOCKS * t + 3)
                    root(M0[:, 0:QR], QR, SSQ, act_f, bufB[:, 0:QR]).then_inc(s_ssz, 1)
                if k == BLOCK_STEP[2] + 1:
                    act.wait_ge(s_rz, t + 1)
                    copy(cqn, M0[:, 0:QR], col(RQ)).then_inc(s_cqn, 1)
                if k == BLOCK_STEP[5]:
                    act.wait_ge(s_wused, BLOCKS * t + 6)
                    root(M1[:, 0:KVR], KVR, SSK, act_f, bufB[:, QR:QR + KVR]).then_inc(s_ssz, 1)
                if k == 14:
                    if first(t):
                        act.wait_ge(s_init, INITS)
                    kv_stage(n, at, 0)
                if k in (13, 15):
                    half = (k - 13) // 2
                    act.wait_ge(s_qps, 2 * t + half + 1)
                    copy(qn[:, half * QR:(half + 1) * QR], Mb[half][:, 0:QR]).then_inc(s_qn, 1)
                if k == 19:
                    kv_stage(n, at, 1)
                if k == 23:
                    kv_stage(n, at, 2)
                for j in range(CC):
                    if k == BLOCK_STEP[NAT_BLOCKS + 3 * j + 2]:
                        act.wait_ge(s_wused, BLOCKS * t + NAT_BLOCKS + 3 * j + 3)
                        copy(csb[:, (j % 2) * P:(j % 2 + 1) * P], Sb[j % 2][:, P:2 * P]).then_inc(s_c, 1)
                if k == 27:
                    act.wait_ge(s_conv, CC * t + CC)
                    act.activation(csq_of(t), conv_v, ACT.Square).then_inc(s_csq, 1)
                if k == 30:
                    act.wait_ge(s_css, t + 1)
                    act.activation(col(SSC), T1[:, 0:1], ACT.Sqrt, bias=col(EPSC), scale=1.0 / CW).then_inc(s_ssc, 1)
                if first(t) and k == FIRST_ATT_STEP:
                    act.wait_ge(s_nm, H)
                    for h in range(H):
                        act.activation(bufA[:, h * P:(h + 1) * P], bufA[:, h * P:(h + 1) * P], ACT.Exp,
                                       bias=nm[:, h:h + 1], scale=SCALE, accum_out=rs[:, h:h + 1]).then_inc(s_p, 1)
                if first(t) and k == FIRST_ATT_STEP + 3:
                    act.wait_ge(s_pTps, 2 * H)
                    copy(bufB[:, 512:1024], T1[:, :]).then_inc(s_pTb, H)
                nk = key_blocks(t) * P
                for h in range(0 if first(t) else H):
                    k0 = ATT_STEP + 4 * h
                    if k == k0:
                        act.wait_ge(s_nm, H * t + h + 1)
                        act.activation(bufA[:, 0:nk], bufA[:, 0:nk], ACT.Exp, bias=nm[:, h:h + 1], scale=SCALE,
                                       accum_out=rs[:, h:h + 1]).then_inc(s_p, 1)
                    if k == k0 + 3 and nk <= 512:
                        act.sem_inc(s_pTb, 1)
                    elif k == k0 + 3:
                        act.wait_ge(s_pTps, 2 * H * t + 2 * h + 2)
                        if h > 0:
                            act.wait_ge(s_pv, H * t + h)
                        copy(bufB[:, 512:1024], T1[:, :]).then_inc(s_pTb, 1)
                if k == 63:
                    act.wait_ge(s_at, t + 1)
                    root(attn[:, :], CW, SSA, act_f, bufB[:, 0:CW]).then_inc(s_ssa, 1)
                if k == 74:
                    act.wait_ge(s_xm, 2 * t + 2)
                    root(x_front[:, :], D, SSM, act_f, bufB[:, :]).then_inc(s_ssm, 1)
                if k == 78:
                    for half in range(2):
                        act.wait_ge(s_hfps, 2 * t + half + 1)
                        copy(actT[:, half * 512:(half + 1) * 512], Tb[half][:, :]).then_inc(s_hfT, 1)
                for b in range(PQ_BLOCKS):
                    if k == BLOCK_STEP[IN_BLOCKS + b]:
                        act.wait_ge(s_wused, BLOCKS * t + IN_BLOCKS + b + 1)
                        if b >= 2:
                            act.wait_ge(s_s, PQ_BLOCKS * t + b - 1)
                        copy(pqT[:, (b % 2) * P:(b % 2 + 1) * P], Mb[b % 2][:, 0:P]).then_inc(s_pqT, 1)
                for h in range(PH):
                    if k == BLOCK_STEP[IN_BLOCKS + 2 * h + 1] + 4:
                        act.wait_ge(s_best, PH * t + h + 1)
                        b = best[:, h * TOPK:(h + 1) * TOPK]
                        act.activation(b, b, ACT.Exp, bias=gsum[:, PH + h:PH + h + 1],
                                       accum_out=gsum[:, h:h + 1]).then_inc(s_ge, 1)

            def hand_x(t):
                act.wait_ge(s_xm, 2 * t + 2)
                if not first(t):
                    act.wait_ge(s_x2, 1 * t)
                copy(x_peer[:, :], x_front[:, :]).then_inc(s_handx, 1)

            def slot(t, before, k, gates, eye, rows):
                if k % TOPK == 0:
                    act.wait_ge(s_gate, PH * (t + 1) if sample(t) else PH * t + k // TOPK + 1)
                act.wait_ge(s_dot, before + k + 1)
                act_p.link(act, act.activation(dots[:, k:k + 1], dots[:, k:k + 1], ACT.Gelu))
                act_p.link(act, copy(dots[:, k:k + 1], dots[:, k:k + 1], gates[:, k:k + 1]))
                act.wait_ge(s_slot, before + k + RING - 1)
                copy(diag[:, (k % 2) * P:(k % 2) * P + rows], eye, dots[:, k:k + 1]).then_inc(s_diag, 1)

            def finish(t):
                act.wait_ge(s_x2, t + 1)
                act_y.start(t)
                root(y_buf[:, :], D, SS2, act_y, x_peer[:, :]).then_inc(s_ss2, 1)

            def body(t):
                act_p.start(t)
                for k in range(SLOTS + LAG):
                    if k < SLOTS:
                        slot(t, SLOTS * t, k, gate_peer, ident[:, :], P)
                    if k == 1:
                        if not first(t):
                            finish(t - 1)
                        hand_x(t)
                    if k >= LAG:
                        for tile, step in front_steps(t, k - LAG):
                            front(tile, step)
                act_p.end()

            for k in range(FS_FIRST):
                front(0, k)
            body(0)
            with act.Fori(1, TILES - 1) as t:
                body(t)
            body(TILES - 1)
            act.wait_ge(s_pack, 16 * 3 * PACK)
            act_p.start(TILES)
            act.wait_ge(s_fold, PACK)
            for k in range(PSLOTS):
                slot(S_TILE, SLOTS * TILES, k, gate_pack, fold[:, :], DEC)
                if k == 1:
                    finish(TILES - 1)
                    hand_x(S_TILE)
            finish(S_TILE)

        @block.vector
        def _(dve):
            def rstd(c_ss, c_r):
                return dve.reciprocal(col(c_r), col(c_ss))

            def rotate(x, out, n, link):
                c = rope[:, 0:HALF].unsqueeze(1).to_broadcast([P, n, HALF])
                s = rope[:, HALF:ROPE].unsqueeze(1).to_broadcast([P, n, HALF])
                r = [rtmp[:, i * H * HALF:i * H * HALF + n * HALF].rearrange("p (h c) -> p h c", h=n) for i in range(4)]
                x1, x2 = x[:, :, 0:HALF], x[:, :, HALF:ROPE]
                dve.tensor_tensor(r[0], x1, c, ALU.mult)
                dve.tensor_tensor(r[1], x2, s, ALU.mult)
                dve.tensor_tensor(r[2], x1, s, ALU.mult)
                link(dve.tensor_tensor(r[3], x2, c, ALU.mult))
                dve.tensor_tensor(out[:, :, 0:HALF], r[0], r[1], ALU.subtract)
                return dve.tensor_tensor(out[:, :, HALF:ROPE], r[2], r[3], ALU.add)

            def kv_stage(n):
                dve.wait_ge(s_ckps, n + 1)
                dve.tensor_copy(ckT, T1[:, 0:KVR]).then_inc(s_ckT, 1)

            def top16(vals, idx, src, rest, link):
                link(dve.max(vals[:, 0:8], src))
                dve.max_index(idx[:, 0:8], vals[:, 0:8], src)
                link(dve.match_replace(rest, vals[:, 0:8], src, LOWEST))
                link(dve.max(vals[:, 8:16], rest))
                return dve.max_index(idx[:, 8:16], vals[:, 8:16], rest)

            def front(t, k):
                n = S_TILE + 2 if sample(t) else t

                def link(ins):
                    dve_f.link(dve, ins)

                def link_apart(ins):
                    dve_f.link(dve, ins, wait_apart)

                if k == 1:
                    dve.wait_ge(s_ssx, t + 1)
                    rstd(SSX, RX).then_inc(s_rx, 1)
                    if first(t):
                        dve.memset(uT_v[:, :, 0:CK - 1], 0.0).then_inc(s_carry, 1)
                    elif sample(t):
                        dve.tensor_copy(convp[:, :].rearrange("p (j n) -> p j n", j=CC), uT_v[:, :, P:P + CK - 1])
                        dve.tensor_copy(uT_v[:, :, 0:CK - 1], state_v).then_inc(s_carry, 1)
                    else:
                        dve.tensor_copy(uT_v[:, :, 0:CK - 1], uT_v[:, :, P:P + CK - 1]).then_inc(s_carry, 1)
                    if sample(t):
                        dve.tensor_copy(mask[:, 0:PAST + DEC],
                                        zeros[:, 0:1].to_broadcast([P, PAST + DEC]))
                        dve.memset(mask[:, PAST + DEC:KEYS], NEG).then_inc(s_mask, 1)
                    else:
                        if first(t):
                            dve.wait_ge(s_init, SMALL_INITS)
                            dve.tensor_copy(mask[:, 0:P], mask_tile[:, :]).then_inc(s_mask, 1)
                        else:
                            dve.tensor_copy(mask[:, bass.ds((t - 1) * P, P)], zeros[:, :])
                            dve.tensor_copy(mask[:, bass.ds(t * P, P)], mask_tile[:, :]).then_inc(s_mask, 1)
                if k == 3:
                    if first(t):
                        dve.wait_ge(s_const, 16 * 2)
                    for half in range(2):
                        dve.wait_ge(s_hps, 2 * t + half + 1)
                        dve.tensor_tensor(actT_v[:, 4 * half:4 * half + 4, :], v3(Tb[half][:, :], 4),
                                          gain(C_GATTN + 4 * half, 4), ALU.mult).then_inc(s_hT, 1)
                if k == BLOCK_STEP[2] + 1:
                    dve.wait_ge(s_ssz, 2 * t + 1)
                    rstd(SSQ, RQ).then_inc(s_rz, 1)
                if sample(t):
                    for b, part in PAST_STEPS.get(k, ()):
                        if part == 0:
                            kv_stage(TILES + b)
                if k == 10:
                    if not (first(t) or first(t - 1)):
                        dve.wait_ge(s_yst, 16 * (t - 1))
                    dve.wait_ge(s_cqps, t + 1)
                    dve.tensor_tensor(v3(cqT, QC), v3(T0[:, 0:QR], QC), gain(C_GQ, QC), ALU.mult).then_inc(s_cqT, 1)
                if k == BLOCK_STEP[5] + 1:
                    dve.wait_ge(s_ssz, 2 * t + 2)
                    link(rstd(SSK, RK))
                    dve.wait_ge(s_rope, 16 * (t + 1))
                    if not first(t):
                        dve.wait_ge(s_kvst, 32 * t)
                    dve.scalar_tensor_tensor(out=ckn[:, 0:KVR], in0=M1[:, 0:KVR], scalar=col(RK), in1=g_kv[:, :],
                                             op0=ALU.mult, op1=ALU.mult)
                    rotate(M1[:, KVR:KVR + ROPE].unsqueeze(1), ckn[:, KVR:KVR + ROPE].unsqueeze(1), 1,
                           link).then_inc(s_ckn, 1)
                if k == 14:
                    kv_stage(n)
                if k == 16:
                    dve.wait_ge(s_qn, 2 * t + 2)
                    pe_part = qn.rearrange("p (h c) -> p h c", h=H)[:, :, NOPE:QK]
                    rotate(pe_part, pe_part, H, link).then_inc(s_qr, 1)
                    dve.wait_ge(s_qr, t + 1)
                    dve.tensor_copy(rtmp[:, 0:1], rope[:, 0:1]).then_inc(s_ropeb, 1)
                if k == (FIRST_ATT_STEP if first(t) else 26):
                    dve.wait_ge(s_kvps, 3 * n + 3)
                    for half in range(2):
                        dve.wait_ge(s_qTps, 2 * t + half + 1)
                        dve.tensor_copy(qT[0:QK, half * 512:(half + 1) * 512], Mb[half][0:QK, :]).then_inc(s_qT, 1)
                for j in range(CC):
                    if k == BLOCK_STEP[NAT_BLOCKS + 3 * j + 2] + 1:
                        dve.wait_ge(s_c, CC * t + j + 1)
                        u, o = uT_v[:, j, :], conv_v[:, j, :]
                        w = [cols[:, C_WCONV + CC * i + j:C_WCONV + CC * i + j + 1] for i in range(CK)]
                        link(dve.tensor_tensor(u[:, CK - 1:CK - 1 + P], Sb[j % 2][:, 0:P],
                                               csb[:, (j % 2) * P:(j % 2 + 1) * P], ALU.mult))
                        link(dve.tensor_scalar(o, u[:, 0:P], w[0], None, ALU.mult))
                        for i in (1, 2):
                            link(dve.scalar_tensor_tensor(out=o, in0=u[:, i:i + P], scalar=w[i], in1=o,
                                                          op0=ALU.mult, op1=ALU.add))
                        dve.tensor_tensor(o, o, Sb[j % 2][:, 2 * P:3 * P], ALU.mult).then_inc(s_conv, 1)
                if k == 28:
                    dve.wait_ge(s_conv, CC * t + CC)
                    dve.tensor_tensor(actT_v[:, 4:8, :], conv_v, gain(C_GCONV, CC), ALU.mult).then_inc(s_mixc, 1)
                if k == 31:
                    dve.wait_ge(s_ssc, t + 1)
                    rstd(SSC, RC).then_inc(s_rc, 1)
                if first(t) and k == FIRST_ATT_STEP:
                    dve.wait_ge(s_sc, H)
                    dve.tensor_tensor(v3(bufA[:, :], H), v3(acc[:, :], H),
                                      mask_tile[:, :].unsqueeze(1).to_broadcast([P, H, P]), ALU.add).then_inc(s_sm, 1)
                    dve.wait_ge(s_sm, 1)
                    dve.tensor_reduce(mx[:, :], v3(bufA[:, :], H), AX.X, ALU.max).then_inc(s_sm, H - 1)
                    dve.wait_ge(s_sm, H)
                    dve.tensor_scalar(nm[:, :], mx[:, :], -SCALE, None, ALU.mult).then_inc(s_nm, H)
                if first(t) and k == FIRST_ATT_STEP + 3:
                    dve.wait_ge(s_pTps, H)
                    dve.tensor_copy(bufB[:, 0:512], T0[:, :]).then_inc(s_pTa, H)
                for h in range(0 if first(t) else H):
                    k0 = ATT_STEP + 4 * h
                    if k == k0:
                        dve.wait_ge(s_sc, H * t + h + 1)
                        if h == 0:
                            wait_apart(dve, s_mask, t + 1)
                        else:
                            wait_apart(dve, s_pTps, 2 * H * t + 2 * h)
                        nk = key_blocks(t) * P
                        dve.tensor_tensor_reduce(bufA[:, 0:nk], Sps[:, 0:nk], mask[:, 0:nk], 1.0, LOWEST, ALU.add, ALU.max,
                                                 mx[:, h:h + 1]).then_inc(s_sm, 1)
                        dve.wait_ge(s_sm, H * t + h + 1)
                        dve.tensor_scalar(nm[:, h:h + 1], mx[:, h:h + 1], -SCALE, None, ALU.mult).then_inc(s_nm, 1)
                    if k == k0 + 3:
                        dve.wait_ge(s_pTps, 2 * H * t + 2 * h + 1)
                        if h > 0:
                            dve.wait_ge(s_pv, H * t + h)
                        n_low = min(512, key_blocks(t) * P)
                        dve.tensor_copy(bufB[:, 0:n_low], T0[:, 0:n_low]).then_inc(s_pTa, 1)
                if k == 62:
                    dve.wait_ge(s_pv, H * t + H)
                    link(dve.reciprocal(ri[:, :], rs[:, :]))
                    dve.tensor_tensor(attn[:, :].rearrange("p (h c) -> p h c", h=H),
                                      M1[:, :].rearrange("p (h c) -> p h c", h=H),
                                      ri[:, :].unsqueeze(2).to_broadcast([P, H, VD]), ALU.mult).then_inc(s_at, 1)
                if k == 65:
                    dve.wait_ge(s_ssa, t + 1)
                    link(rstd(SSA, RA))
                    dve.wait_ge(s_aps, t + 1)
                    dve.tensor_tensor(actT_v[:, 0:4, :], v3(T0[:, :], 4), gain(C_GMLA, 4), ALU.mult).then_inc(s_mixa, 1)
                if k in (WOUT_STEPS[1], WOUT_STEPS[3]):
                    half = k // WOUT_STEPS[3]
                    x = x_front[:, half * 512:(half + 1) * 512]
                    for i, c in ((0, RA), (1, RC)):
                        if first(t):
                            dve.wait_ge(s_wo, 2 + half + 1)
                            bank = (S0[:, :], acc[:, 0:512], T1[:, :], acc[:, 512:1024])[2 * half + i]
                        else:
                            dve.wait_ge(s_wo, 4 * t + 2 * half + i + 1)
                            bank = (S0, S1, T1, M0)[2 * half + i][:, :]
                        ins = dve.scalar_tensor_tensor(out=x, in0=bank, scalar=col(c),
                                                       in1=x, op0=ALU.mult, op1=ALU.add)
                        if i == 0:
                            link(ins)
                        else:
                            ins.then_inc(s_xm, 1)
                if k == 75:
                    dve.wait_ge(s_ssm, t + 1)
                    if first(t):
                        dve.wait_ge(s_late, 16 * 4)
                    link(rstd(SSM, RM))
                    dve.scalar_tensor_tensor(out=hf_front[:, :], in0=x_front[:, :], scalar=col(RM), in1=g_ffn[:, :],
                                             op0=ALU.mult, op1=ALU.mult).then_inc(s_hf, 1)
                for b in range(PQ_BLOCKS):
                    if k == BLOCK_STEP[IN_BLOCKS + b] + 3:
                        wait_apart(dve, s_s, PQ_BLOCKS * t + b + 1)
                        top16(tv[:, b * TOPK:(b + 1) * TOPK], ti[:, b * TOPK:(b + 1) * TOPK],
                              Sb[b % 2][:, 0:P], s2, link_apart).then_inc(s_l1, 1)
                for h in range(PH):
                    if k == BLOCK_STEP[IN_BLOCKS + 2 * h + 1] + 4:
                        dve.wait_ge(s_l1, PQ_BLOCKS * t + 2 * h + 2)
                        va, vb = (tv[:, (2 * h + i) * TOPK:(2 * h + i + 1) * TOPK] for i in range(2))
                        dve.tensor_tensor(cand.rearrange("p (a b) -> p a b", a=TOPK),
                                          va.unsqueeze(2).to_broadcast([P, TOPK, TOPK]),
                                          vb.unsqueeze(1).to_broadcast([P, TOPK, TOPK]), ALU.add)
                        link_apart(dve.tensor_copy(tif[:, :], ti[:, 2 * h * TOPK:(2 * h + 2) * TOPK]))
                        link(top16(best[:, h * TOPK:(h + 1) * TOPK], pos, cand, cand2, link_apart))
                        dve.tensor_scalar(gsum[:, PH + h:PH + h + 1], best[:, h * TOPK:h * TOPK + 1], -1.0, None,
                                          ALU.mult).then_inc(s_best, 1)
                        dve.tensor_scalar(pab[:, 0:TOPK], pos[:, :], 4, None, ALU.logical_shift_right)
                        link(dve.tensor_scalar(pab[:, TOPK:2 * TOPK], pos[:, :], TOPK - 1, None, ALU.bitwise_and))
                        link(dve.tensor_copy(pabf[:, :], pab[:, :]))
                    if k == BLOCK_STEP[IN_BLOCKS + 2 * h + 1] + 5:
                        for i in range(2):
                            link(dve.tensor_tensor(hot, pabf[:, i * TOPK:(i + 1) * TOPK].unsqueeze(2).to_broadcast([P, TOPK, TOPK]),
                                                   iota16[:, :].unsqueeze(1).to_broadcast([P, TOPK, TOPK]), ALU.is_equal))
                            link(dve.tensor_tensor(hot, hot, tif[:, i * TOPK:(i + 1) * TOPK].unsqueeze(1).to_broadcast([P, TOPK, TOPK]),
                                                   ALU.mult))
                            link(dve.tensor_reduce(eab[:, i * TOPK:(i + 1) * TOPK], hot, AX.X, ALU.add))
                        link(dve.scalar_tensor_tensor(out=pabf[:, 0:TOPK], in0=eab[:, 0:TOPK], scalar=float(NKEYS),
                                                      in1=eab[:, TOPK:2 * TOPK], op0=ALU.mult, op1=ALU.add))
                        if sample(t):
                            dst = idx_s[:, h * TOPK:(h + 1) * TOPK]
                        else:
                            dst = (idx_peer if h else idx_lead)[:, h * TOPK:(h + 1) * TOPK]
                        dve.tensor_copy(dst, pabf[:, 0:TOPK]).then_inc(s_idx, 1)
                    if k == BLOCK_STEP[IN_BLOCKS + 2 * h + 1] + 7:
                        dve.wait_ge(s_ge, PH * t + h + 1)
                        link(dve.reciprocal(gsum[:, PH + h:PH + h + 1], gsum[:, h:h + 1]))
                        dve.tensor_scalar((gate_s if sample(t) else gate_peer)[:, h * TOPK:(h + 1) * TOPK],
                                          best[:, h * TOPK:(h + 1) * TOPK], gsum[:, PH + h:PH + h + 1], None,
                                          ALU.mult).then_inc(s_gate, 1)

            def whole_front(t, k):
                dve_f.start(t, k)
                front(t, k)
                if k == STEPS - 1:
                    dve_f.end()

            def hand(t):
                dve.wait_ge(s_hf, t + 1)
                if not first(t):
                    dve.wait_ge(s_dot, SLOTS * t)
                dve.tensor_copy(hf_peer[:, :], hf_front[:, :]).then_inc(s_handh, 1)
                dve.wait_ge(s_handh, t + 1)

            def slot(t, k, hf):
                dve.wait_ge(s_gu[k % RING], 16 * ((SLOTS // RING) * t + k // RING + 1))
                u = ring_u[k % RING][:, :]
                dve.tensor_tensor_reduce(u, u, hf[:, :], 1.0, 0.0, ALU.mult, ALU.add,
                                         dots[:, k:k + 1]).then_inc(s_dot, 1)

            def add_experts(t):
                rows = slice(0, DEC if sample(t) else P)
                dve.wait_ge(s_slot, RING + SLOTS * TILES + PSLOTS if sample(t) else SLOTS * t + SLOTS + RING)
                dve.wait_ge(s_handx, t + 1)
                if not first(t):
                    dve.wait_ge(s_yst, 16 * t)
                dve.tensor_tensor(y_buf[rows, :], x_peer[rows, :], acc[rows, :], ALU.add).then_inc(s_x2, 1)

            def finish(t):
                rows = slice(0, DEC if sample(t) else P)
                dve_y.start(t)
                dve.wait_ge(s_ss2, t + 1)
                dve_y.link(dve, rstd(SS2, R2))
                dve_y.link(dve, dve.scalar_tensor_tensor(out=y_buf[rows, :], in0=y_buf[rows, :],
                                                         scalar=st[rows, R2:R2 + 1], in1=g_fin[rows, :],
                                                         op0=ALU.mult, op1=ALU.mult))
                dve.sem_inc(s_y, 1)
                dve_y.end()

            def body(t):
                hand(t)
                for k in range(SLOTS + LAG):
                    if k < SLOTS:
                        slot(t, k, hf_peer)
                    if k == 0 and not first(t):
                        add_experts(t - 1)
                    if k == 4 and not first(t):
                        finish(t - 1)
                    if k >= LAG:
                        for tile, step in front_steps(t, k - LAG):
                            whole_front(tile, step)

            for k in range(FS_FIRST):
                whole_front(0, k)
            for q in range(PACK):
                group = slice(q * DEC, (q + 1) * DEC)
                dve.tensor_copy(fold[group, :], ident[group, group]).then_inc(s_fold, 1)
            body(0)
            with dve.Fori(1, TILES - 1) as t:
                body(t)
            body(TILES - 1)
            dve.wait_ge(s_pack, 16 * 3 * PACK)
            for k in range(PSLOTS):
                slot(TILES, k, hf_pack)
                if k == 0:
                    add_experts(TILES - 1)
                if k == 4:
                    finish(TILES - 1)
            add_experts(S_TILE)
            finish(S_TILE)



def blocks(w):
    k, n = w.shape
    return w.reshape(k // P, P, n // P, P).transpose(2, 1, 0, 3).reshape(n // P, P, -1)


def rows(w):
    k, n = w.shape
    return w.reshape(k // P, P, n).transpose(1, 0, 2).reshape(P, -1)


def rope_table():
    at = np.concatenate([np.arange(SEQ), PAST + np.arange(P)]).astype(np.float32)
    freqs = np.float32(10000.0) ** (-np.arange(HALF, dtype=np.float32) / HALF)
    ang = at[:, None] * freqs[None, :].astype(np.float32)
    return np.concatenate([np.cos(ang), np.sin(ang)], axis=1).astype(np.float32)


def kernel(**inputs):
    import concourse.bacc as bacc
    from concourse.bass_utils import run_bass_kernel_spmd

    v = {n: np.asarray(x) for n, x in inputs.items()}
    w_in = v["w_in"][0]
    u0, b0, c0 = NATW, NATW + CW, NATW + 2 * CW
    order = [w_in[:, i * P:(i + 1) * P] for i in range(NAT_BLOCKS - 1)]
    for j in range(CC):
        order += [w_in[:, o + j * P:o + (j + 1) * P] for o in (u0, c0, b0)]
    col = lambda g: g.reshape(-1, P).T
    arrays = {
        "x_p": v["x_prompt"][0],
        "x_s": v["x_sample"][0],
        "c_kv": v["cache_kv_latent"][0, 0],
        "c_pe": v["cache_k_rope"][0, 0],
        "rope": rope_table(),
        "w_blocks": np.concatenate([blocks(np.concatenate(order, axis=1)), blocks(v["w_peer_q"][0])]),
        "w_narrow": rows(w_in[:, NATW - ROPE:NATW]),
        "w_uq": rows(v["w_uq"][0]),
        "w_ukv": rows(v["w_ukv"][0]),
        "w_out": rows(v["w_out"][0]),
        "keysT": v["peer_keys"][0].transpose(3, 0, 1, 2).reshape(P, -1),
        "g_ffn": v["g_ffn_norm"][0],
        "g_fin": v["g_final"],
        "g_kv": v["g_kv"][0],
        "cols": np.concatenate([col(v["g_attn_norm"][0]), col(v["g_q"][0]), col(v["g_mla_out"][0]),
                                col(v["g_conv_out"][0]), *[col(w) for w in v["w_conv"][0]],
                                v["state_conv"][0, 0].reshape(CK - 1, CC, P).transpose(2, 1, 0).reshape(P, -1)],
                               axis=1),
        "peer_u": v["peer_u"][0],
        "peer_v": v["peer_v"][0],
    }
    outs = {
        "o_y_p": (SEQ, D), "o_y_s": (DEC, D), "o_kv_p": (SEQ, KVR), "o_pe_p": (SEQ, ROPE),
        "o_kv_s": (DEC, KVR), "o_pe_s": (DEC, ROPE), "o_cv_p": (P, CC * (CK - 1)), "o_cv_s": (P, CC * (CK - 1)),
    }
    nc = bacc.Bacc("TRN2", target_bir_lowering=False, num_devices=1,
                   dynamic_dma_scratch_size=8192)
    arrays = {n: np.ascontiguousarray(x) for n, x in arrays.items()}
    a = {n: nc.dram_tensor(f"in_{n}", x.shape, F32, kind="ExternalInput").ap() for n, x in arrays.items()}
    a |= {n: nc.dram_tensor(n, s, F32, kind="ExternalOutput").ap() for n, s in outs.items()}
    build(nc, a)
    r = run_bass_kernel_spmd(nc, [{f"in_{n}": x for n, x in arrays.items()}], core_ids=[0]).results[0]
    conv = lambda x: x.reshape(P, CC, CK - 1).transpose(2, 1, 0).reshape(1, 1, CK - 1, CW)
    return (r["o_y_p"].reshape(1, SEQ, D), r["o_y_s"].reshape(1, DEC, D), r["o_kv_p"].reshape(1, 1, SEQ, KVR),
            r["o_pe_p"].reshape(1, 1, SEQ, ROPE), conv(r["o_cv_p"]), r["o_kv_s"].reshape(1, 1, DEC, KVR),
            r["o_pe_s"].reshape(1, 1, DEC, ROPE), conv(r["o_cv_s"]))
```
